# Optimizing a Trainium2 kernel written in Bass

```python
import math
import jax, jax.numpy as jnp
from jax import lax
import numpy as np

D_MODEL = 1024
BATCH = 1
SEQ = 256
DEPTH = 2

GRID_W = 64
CTX_LEN = 256
N_MOD = 6
EPS = 1e-6

D_CONV = D_MODEL // 2
CONV_WIDTH = 31
D_POOL = D_MODEL // 2
POOL_WINDOWS = (2, 4, 8, 16)
POOL_GROUP = D_POOL // len(POOL_WINDOWS)
EVEN_IN = 2 * D_CONV + D_POOL
EVEN_MIX = D_CONV + D_POOL

MLA_HEADS = 4
Q_LORA = D_MODEL // 4
KV_LORA = D_MODEL // 8
QK_NOPE = 128
QK_ROPE = 64
V_HEAD = 128
DIFF_HEADS = 4
DIFF_QK = 64
DIFF_V = 128
DIFF_QK_COLS = DIFF_HEADS * 2 * DIFF_QK
Q_COLS = Q_LORA + DIFF_QK_COLS
KV_COLS = KV_LORA + QK_ROPE + DIFF_QK_COLS + DIFF_HEADS * DIFF_V
ODD_IN = Q_COLS + KV_COLS
ODD_MIX = MLA_HEADS * V_HEAD + DIFF_HEADS * DIFF_V
MLA_SCALE = (QK_NOPE + QK_ROPE) ** -0.5
DIFF_SCALE = DIFF_QK ** -0.5
ROPE_BASE = 10000.0
Q_BLOCK = 128

N_EXPERTS = 32
N_GROUPS = 8
EXPERTS_PER_GROUP = N_EXPERTS // N_GROUPS
TOP_K = 2
D_EXPERT = 256

N_EVEN = (DEPTH + 1) // 2
N_ODD = DEPTH // 2

kernel_name = "hybrid_conv_pool_mla_diffattn_moe_dit"

def rms_norm(x, g):
    xf = x.astype(jnp.float32)
    y = xf * lax.rsqrt(jnp.mean(xf * xf, axis=-1, keepdims=True) + EPS)
    return (y * g).astype(x.dtype)

def layer_norm(x, g, b):
    xf = x.astype(jnp.float32)
    mu = jnp.mean(xf, axis=-1, keepdims=True)
    xc = xf - mu
    y = xc * lax.rsqrt(jnp.mean(xc * xc, axis=-1, keepdims=True) + EPS)
    return (y * g + b).astype(x.dtype)

def modulate(h, shift, scale):
    return h * (1.0 + scale) + shift

def axial_rope_tables(rows, rot_dim):
    row = jnp.repeat(jnp.arange(rows, dtype=jnp.float32), GRID_W)
    col = jnp.tile(jnp.arange(GRID_W, dtype=jnp.float32), rows)
    axis_dim = rot_dim // 2
    inv_freq = ROPE_BASE ** (-jnp.arange(0, axis_dim, 2, dtype=jnp.float32) / axis_dim)
    ang = jnp.concatenate([row[:, None] * inv_freq, col[:, None] * inv_freq], axis=-1)
    return jnp.cos(ang), jnp.sin(ang)

def apply_rope(x, cos, sin):
    half = x.shape[-1] // 2
    shape = (1, x.shape[1]) + (1,) * (x.ndim - 3) + (half,)
    cs = cos.reshape(shape).astype(x.dtype)
    sn = sin.reshape(shape).astype(x.dtype)
    x1, x2 = x[..., :half], x[..., half:]
    return jnp.concatenate([x1 * cs - x2 * sn, x2 * cs + x1 * sn], axis=-1)

def attend(q, k, v, scale):
    b, lq, h, dk = q.shape
    nb = lq // Q_BLOCK
    qb = jnp.moveaxis(q.reshape(b, nb, Q_BLOCK, h, dk), 1, 0)

    def one_block(qi):
        s = jnp.einsum('bqhd,bkhd->bhqk', qi, k).astype(jnp.float32) * scale
        p = jax.nn.softmax(s, axis=-1).astype(v.dtype)
        return jnp.einsum('bhqk,bkhd->bqhd', p, v)

    out = lax.map(one_block, qb)
    return jnp.moveaxis(out, 0, 1).reshape(b, lq, h, v.shape[-1])

def conformer_conv(u, dw_w, dw_b, ln_g, ln_b):
    a, g = jnp.split(u, 2, axis=-1)
    y = a * jax.nn.sigmoid(g)
    y = lax.conv_general_dilated(
        y, dw_w[:, None, :], window_strides=(1,),
        padding=[(CONV_WIDTH // 2, CONV_WIDTH // 2)],
        dimension_numbers=('NWC', 'WIO', 'NWC'),
        feature_group_count=D_CONV) + dw_b
    return jax.nn.silu(layer_norm(y, ln_g, ln_b))

def centred_mean_minus_self(x, w):
    n = x.shape[1]
    xf = x.astype(jnp.float32)
    cs = jnp.concatenate([jnp.zeros_like(xf[:, :1]), jnp.cumsum(xf, axis=1)], axis=1)
    t = jnp.arange(n)
    lo = jnp.clip(t - w // 2, 0, n)
    hi = jnp.clip(t + w // 2, 0, n)
    cnt = (hi - lo).astype(jnp.float32)[None, :, None]
    return ((cs[:, hi] - cs[:, lo]) / cnt - xf).astype(x.dtype)

def pool_mix(u, pool_w, pool_scale):
    groups = [centred_mean_minus_self(u[..., g * POOL_GROUP:(g + 1) * POOL_GROUP], w)
              for g, w in enumerate(POOL_WINDOWS)]
    y = jnp.stack(groups, axis=2)
    y = jnp.einsum('blgc,gcd->blgd', y, pool_w).reshape(u.shape)
    return y * pool_scale

def even_mixer(h, w_in, dw_w, dw_b, ln_g, ln_b, pool_w, pool_scale, w_out):
    u = h @ w_in
    y_conv = conformer_conv(u[..., :2 * D_CONV], dw_w, dw_b, ln_g, ln_b)
    y_pool = pool_mix(u[..., 2 * D_CONV:], pool_w, pool_scale)
    return jnp.concatenate([y_conv, y_pool], axis=-1) @ w_out

def rope_tail(x, rope):
    return jnp.concatenate([x[..., :QK_NOPE], apply_rope(x[..., QK_NOPE:], *rope)], axis=-1)

def odd_queries(p_q, g_cq, w_uq, g_q_mla, g_q_diff, rope):
    b, l, _ = p_q.shape
    c_q = rms_norm(p_q[..., :Q_LORA], g_cq)
    q_m = rms_norm((c_q @ w_uq).reshape(b, l, MLA_HEADS, QK_NOPE + QK_ROPE), g_q_mla)
    q_d = rms_norm(p_q[..., Q_LORA:].reshape(b, l, DIFF_HEADS, 2, DIFF_QK), g_q_diff)
    if rope is not None:
        q_m = rope_tail(q_m, rope)
        q_d = apply_rope(q_d, *rope)
    return (q_m, q_d[..., 0, :], q_d[..., 1, :])

def odd_keys_values(p_kv, g_ckv, w_ukv, g_k_mla, g_k_diff, rope):
    b, l, _ = p_kv.shape
    c_kv = rms_norm(p_kv[..., :KV_LORA], g_ckv)
    k_rope = p_kv[..., KV_LORA:KV_LORA + QK_ROPE]
    off = KV_LORA + QK_ROPE
    k_d = p_kv[..., off:off + DIFF_QK_COLS].reshape(b, l, DIFF_HEADS, 2, DIFF_QK)
    v_d = p_kv[..., off + DIFF_QK_COLS:].reshape(b, l, DIFF_HEADS, DIFF_V)
    kv = (c_kv @ w_ukv).reshape(b, l, MLA_HEADS, QK_NOPE + V_HEAD)
    k_nope, v_m = kv[..., :QK_NOPE], kv[..., QK_NOPE:]
    k_m = jnp.concatenate(
        [k_nope, jnp.broadcast_to(k_rope[:, :, None, :], (b, l, MLA_HEADS, QK_ROPE))], axis=-1)
    k_m = rms_norm(k_m, g_k_mla)
    k_d = rms_norm(k_d, g_k_diff)
    if rope is not None:
        k_m = rope_tail(k_m, rope)
        k_d = apply_rope(k_d, *rope)
    return (k_m, v_m, k_d[..., 0, :], k_d[..., 1, :], v_d)

def odd_output(qs, kvs, lam, lam_init, g_sub, w_out):
    q_m, q1, q2 = qs
    k_m, v_m, k1, k2, v_d = kvs
    b, l = q_m.shape[:2]
    o_m = attend(q_m, k_m, v_m, MLA_SCALE)
    a1 = attend(q1, k1, v_d, DIFF_SCALE)
    a2 = attend(q2, k2, v_d, DIFF_SCALE)
    o_d = rms_norm(a1 - lam.astype(a1.dtype) * a2, g_sub) * (1.0 - lam_init)
    return jnp.concatenate([o_m.reshape(b, l, -1), o_d.reshape(b, l, -1)], axis=-1) @ w_out

def moe(h, router_w, router_b, w_gate, w_up, w_down):
    scores = jax.nn.sigmoid(jnp.einsum('bld,de->ble', h, router_w).astype(jnp.float32))
    biased = scores + router_b.astype(jnp.float32)
    grp = biased.reshape(biased.shape[:-1] + (N_GROUPS, EXPERTS_PER_GROUP))
    grp_score = lax.top_k(grp, TOP_K)[0].sum(-1)
    sel = jnp.argmax(grp_score, axis=-1)
    in_group = (jnp.arange(N_EXPERTS) // EXPERTS_PER_GROUP) == sel[..., None]
    _, idx = lax.top_k(jnp.where(in_group, biased, -jnp.inf), TOP_K)
    w = jnp.take_along_axis(scores, idx, axis=-1)
    w = w / jnp.sum(w, axis=-1, keepdims=True)
    combine = jnp.einsum('blk,blke->ble', w, jax.nn.one_hot(idx, N_EXPERTS, dtype=jnp.float32)).astype(h.dtype)
    y = jnp.zeros_like(h)
    for e in range(N_EXPERTS):
        he = jax.nn.silu(h @ w_gate[e]) * (h @ w_up[e])
        y = y + combine[..., e:e + 1] * (he @ w_down[e])
    return y

def setup_inputs(seed: int = 0) -> dict:
    key = jax.random.key(seed)
    keys = jax.random.split(key, 30)
    D = D_MODEL

    def nrm(n, shape, s):
        return s * jax.random.normal(keys[n], shape, jnp.float32)

    return {
        "x": nrm(0, (BATCH, SEQ, D), 1.0),
        "c": nrm(1, (BATCH, D), 1.0),
        "ctx": nrm(2, (BATCH, CTX_LEN, D), 1.0),
        "c_ctx": nrm(3, (D,), 1.0),
        "mod_w": nrm(4, (DEPTH, D, N_MOD * D), 0.5 * D ** -0.5),
        "mod_b": nrm(5, (DEPTH, N_MOD * D), 0.02),
        "norm_g": 1.0 + nrm(6, (DEPTH, 2, D), 0.1),
        "even_w_in": nrm(7, (N_EVEN, D, EVEN_IN), D ** -0.5),
        "conv_dw_w": nrm(8, (N_EVEN, CONV_WIDTH, D_CONV), CONV_WIDTH ** -0.5),
        "conv_dw_b": nrm(9, (N_EVEN, D_CONV), 0.02),
        "conv_ln_g": 1.0 + nrm(10, (N_EVEN, D_CONV), 0.1),
        "conv_ln_b": nrm(11, (N_EVEN, D_CONV), 0.02),
        "pool_w": nrm(12, (N_EVEN, len(POOL_WINDOWS), POOL_GROUP, POOL_GROUP), POOL_GROUP ** -0.5),
        "pool_scale": 1.0 + nrm(13, (N_EVEN, D_POOL), 0.1),
        "even_w_out": nrm(14, (N_EVEN, EVEN_MIX, D), EVEN_MIX ** -0.5),
        "odd_w_in": nrm(15, (N_ODD, D, ODD_IN), D ** -0.5),
        "mla_g_cq": 1.0 + nrm(16, (N_ODD, Q_LORA), 0.1),
        "mla_w_uq": nrm(17, (N_ODD, Q_LORA, MLA_HEADS * (QK_NOPE + QK_ROPE)), Q_LORA ** -0.5),
        "mla_g_ckv": 1.0 + nrm(18, (N_ODD, KV_LORA), 0.1),
        "mla_w_ukv": nrm(19, (N_ODD, KV_LORA, MLA_HEADS * (QK_NOPE + V_HEAD)), KV_LORA ** -0.5),
        "qk_g_mla": 1.0 + nrm(20, (N_ODD, 2, QK_NOPE + QK_ROPE), 0.1),
        "qk_g_diff": 1.0 + nrm(21, (N_ODD, 2, DIFF_QK), 0.1),
        "diff_lambda": nrm(22, (N_ODD, 4, DIFF_QK), 0.1),
        "diff_sub_g": 1.0 + nrm(23, (N_ODD, DIFF_V), 0.1),
        "odd_w_out": nrm(24, (N_ODD, ODD_MIX, D), ODD_MIX ** -0.5),
        "router_w": nrm(25, (D, N_EXPERTS), D ** -0.5),
        "router_b": nrm(26, (N_EXPERTS,), 0.01),
        "moe_w_gate": nrm(27, (DEPTH, N_EXPERTS, D, D_EXPERT), D ** -0.5),
        "moe_w_up": nrm(28, (DEPTH, N_EXPERTS, D, D_EXPERT), D ** -0.5),
        "moe_w_down": nrm(29, (DEPTH, N_EXPERTS, D_EXPERT, D), D_EXPERT ** -0.5),
    }

def reference(x, c, ctx, c_ctx, mod_w, mod_b, norm_g, even_w_in, conv_dw_w, conv_dw_b, conv_ln_g,
              conv_ln_b, pool_w, pool_scale, even_w_out, odd_w_in, mla_g_cq, mla_w_uq, mla_g_ckv,
              mla_w_ukv, qk_g_mla, qk_g_diff, diff_lambda, diff_sub_g, odd_w_out, router_w, router_b,
              moe_w_gate, moe_w_up, moe_w_down):
    b, n_lat, d = x.shape
    n_ctx = ctx.shape[1]
    rows = n_lat // GRID_W
    rope = axial_rope_tables(rows, QK_ROPE)
    c_act = jax.nn.silu(c)
    c_ctx_act = jax.nn.silu(c_ctx)
    xl, xc = x, ctx
    for i in range(DEPTH):
        ctx_out = i < DEPTH - 1
        j = i // 2
        mod_l = (c_act @ mod_w[i] + mod_b[i]).reshape(b, N_MOD, 1, d)
        mod_c = (c_ctx_act @ mod_w[i] + mod_b[i]).reshape(N_MOD, d)

        hl = modulate(rms_norm(xl, norm_g[i, 0]), mod_l[:, 0], mod_l[:, 1])
        if i % 2 == 0:
            ew = (even_w_in[j], conv_dw_w[j], conv_dw_b[j], conv_ln_g[j], conv_ln_b[j],
                  pool_w[j], pool_scale[j], even_w_out[j])
            yl = even_mixer(hl, *ew)
            if ctx_out:
                hc = modulate(rms_norm(xc, norm_g[i, 0]), mod_c[0], mod_c[1])
                yc = even_mixer(hc, *ew)
        else:
            hc = modulate(rms_norm(xc, norm_g[i, 0]), mod_c[0], mod_c[1])
            lam_init = 0.8 - 0.6 * math.exp(-0.3 * i)
            dl = diff_lambda[j].astype(jnp.float32)
            lam = jnp.exp(jnp.sum(dl[0] * dl[1])) - jnp.exp(jnp.sum(dl[2] * dl[3])) + lam_init
            qg = (mla_g_cq[j], mla_w_uq[j], qk_g_mla[j, 0], qk_g_diff[j, 0])
            kg = (mla_g_ckv[j], mla_w_ukv[j], qk_g_mla[j, 1], qk_g_diff[j, 1])
            og = (lam, lam_init, diff_sub_g[j], odd_w_out[j])
            w_in = odd_w_in[j]
            kv_c = odd_keys_values(hc @ w_in[:, Q_COLS:], *kg, None)
            p_l = hl @ w_in
            kv_l = odd_keys_values(p_l[..., Q_COLS:], *kg, rope)
            kv_all = tuple(jnp.concatenate([kc, kl], axis=1) for kc, kl in zip(kv_c, kv_l))
            yl = odd_output(odd_queries(p_l[..., :Q_COLS], *qg, rope), kv_all, *og)
            if ctx_out:
                yc = odd_output(odd_queries(hc @ w_in[:, :Q_COLS], *qg, None), kv_c, *og)
        xl = xl + mod_l[:, 2] * yl
        if ctx_out:
            xc = xc + mod_c[2] * yc

        h2l = modulate(rms_norm(xl, norm_g[i, 1]), mod_l[:, 3], mod_l[:, 4])
        if ctx_out:
            h2c = modulate(rms_norm(xc, norm_g[i, 1]), mod_c[3], mod_c[4])
            y2 = moe(jnp.concatenate([h2c, h2l], axis=1), router_w, router_b,
                     moe_w_gate[i], moe_w_up[i], moe_w_down[i])
            xc = xc + mod_c[5] * y2[:, :n_ctx]
            xl = xl + mod_l[:, 5] * y2[:, n_ctx:]
        else:
            xl = xl + mod_l[:, 5] * moe(h2l, router_w, router_b, moe_w_gate[i], moe_w_up[i], moe_w_down[i])
    return xl


_drawn_inputs = setup_inputs


def setup_inputs(seed=0):
    import zlib

    import numpy as np

    out = dict(_drawn_inputs(seed))
    spreads = {}
    factors = {'conv_ln_b': 3.119,
     'mla_g_cq': 7.402,
     'mla_g_ckv': 5.979,
     'qk_g_mla': 6.313,
     'qk_g_diff': 3.75,
     'diff_lambda': 8.0,
     'diff_sub_g': 4.272}
    for name, (base, spread) in spreads.items():
        noise = np.random.default_rng([zlib.crc32(name.encode()), seed]).standard_normal(out[name].shape)
        drawn = base * np.exp(spread * noise) if base else spread * noise
        out[name] = __import__('jax').numpy.asarray(drawn.astype(out[name].dtype))
    for name, factor in factors.items():
        out[name] = (out[name] * factor).astype(out[name].dtype)
    return out
```

```python
from contextlib import ExitStack
import math

import numpy as np

import concourse.bass as bass
from concourse import mybir

P = 128
D = 1024
KC = D // P
NT = 4
HALF = 256
TOK = 512
N_MOD = 6
EPS = 1e-6
TAPS = 31
PADC = TAPS // 2
PADP = 8
WINDOWS = (2, 4, 8, 16)
GROUPS = 8
EPG = 4
EXPERTS = 32
DE = 256
ST = 64
RING = 6
LAM_INIT = 0.8 - 0.6 * math.exp(-0.3)
MLA_SCALE = (128 + 64) ** -0.5
DIFF_SCALE = 64 ** -0.5

ALU = mybir.AluOpType
ACT = mybir.ActivationFunctionType
AX = mybir.AxisListType
F32 = mybir.dt.float32
U32 = mybir.dt.uint32
I32 = mybir.dt.int32


def moe_plan(layer):
    tokens = TOK if layer == 0 else HALF
    c = 2 if layer == 0 else 1
    over = (tokens - c * ST) // ST
    return tokens // P, c, over, GROUPS * c + over


CONST = {}
_at = 0
for _name, _w in (("ident", 128), ("lower", 128), ("ones", 128), ("iota64", 128), ("sel", 4), ("sel32", 32), ("tok", 4), ("iota", 32),
                  ("gdown", 8), ("gup", 8), ("thr", 8), ("before", 64), ("tie", 16),
                  ("cos", 64), ("sin", 64), ("half", 4), ("invcnt", 4 * HALF)):
    CONST[_name] = (_at, _at + _w)
    _at += _w
NCONST = _at


def constants():
    a = np.zeros((P, NCONST), np.float32)

    def put(name, v):
        lo, hi = CONST[name]
        a[:, lo:hi] = v

    r = np.arange(P)
    put("ident", np.eye(P))
    put("lower", (r[:, None] < r[None, :]))
    put("ones", 1)
    put("iota64", np.arange(128) % 64)
    put("sel", (r[:, None] // 64 == np.arange(4)[None, :] // 2) & (r[:, None] % 32 == np.arange(4)[None, :] % 2))
    put("sel32", r[:, None] % 32 == np.arange(32)[None, :])
    put("tok", r[:, None] + 128 * np.arange(4)[None, :])
    put("iota", np.arange(32))
    put("gdown", 8 - np.arange(8))
    put("gup", np.arange(8))
    put("thr", 64 * (1 + np.arange(8)))
    put("before", (np.arange(8)[None, :] < np.arange(8)[:, None]).ravel())
    put("tie", (np.arange(4)[None, :] < np.arange(4)[:, None]).ravel())
    t = np.arange(HALF)
    cnt = [np.clip(t + w // 2, 0, HALF) - np.clip(t - w // 2, 0, HALF) for w in WINDOWS]
    put("invcnt", (1.0 / np.stack(cnt)).astype(np.float32).ravel())
    inv = (np.float32(10000.0) ** (-np.arange(0, 32, 2, dtype=np.float32) / np.float32(32))).astype(np.float32)
    row, col = (t // 64).astype(np.float32), (t % 64).astype(np.float32)
    ang = np.concatenate([row[:, None] * inv, col[:, None] * inv], -1)
    put("cos", np.cos(ang).astype(np.float32).reshape(2, P, 32).transpose(1, 0, 2).reshape(P, 64))
    put("sin", np.sin(ang).astype(np.float32).reshape(2, P, 32).transpose(1, 0, 2).reshape(P, 64))
    put("half", -0.5)
    return a


R_MODB, R_NORM = 0, 96
R_TAPS = 128
R_CCTX, R_C, R_DWB, R_LNG, R_LNB, R_PSC, R_GCQ, R_GCKV, R_SUBG, R_QN, R_KN = (
    256, 264, 272, 276, 280, 284, 288, 290, 291, 292, 293)
NROWS3 = 38
B_RB, B_QKM, B_QKD, B_LAM = 0, 32, 416, 544
NB = 800


def stream_plan():
    def pair(L, v):
        return [("mod", L, v, h) for h in (0, 1)]

    out = pair(0, 0) + pair(0, 1)
    out += [("win", j) for j in range(3)]
    for v in (2, 3, 4, 5):
        out += pair(0, v)
    out += [("wout", 0, 0)] + pair(1, 0) + pair(1, 1) + [("wout", 0, 1)]
    for v in (2, 3, 4, 5):
        out += pair(1, v)
    moe0 = len(out)
    for q in range(GROUPS * 2):
        out += [("gu", 0, 2 * q), ("gu", 0, 2 * q + 1), ("down", 0, q)]
    for j in range(5):
        out.append(("oin", j))
    out.append(("lora",))
    out += [("wout", 1, h) for h in (0, 1)]
    moe1 = len(out)
    for q in range(GROUPS * 2):
        out += [("gu", 1, 2 * q), ("gu", 1, 2 * q + 1), ("down", 1, q)]
    return out, (moe0, moe1)


OIN = [(960, 1472), (1472, 1984), (768, 960), (0, 256), (256, 768)]


def generator_kernel(nc, a, out):
    STREAM, MOE_AT = stream_plan()
    where = {u: n for n, u in enumerate(STREAM)}
    with ExitStack() as ctx:
        def sb(name, shape, dt=F32):
            return ctx.enter_context(nc.sbuf_tensor(name, shape, dt))

        sems = {}

        def sem(name):
            if name not in sems:
                sems[name] = ctx.enter_context(nc.semaphore(name))
            return sems[name]

        cst = sb("cst", [P, NCONST - 4 * HALF])
        par = sb("par", [P, 294])
        brow = sb("brow", [P, NB])
        cs = sb("cs", [P, KC, 32])
        csg = sb("csg", [P, 16])
        mods = sb("mods", [P, 2, N_MOD, KC, 2])
        gsc = sb("gsc", [P, 2, 2, KC, 2])
        rw = sb("rw", [P, KC, EXPERTS])
        pw = sb("pw", [P, 4, P])
        X = sb("X", [P, NT, D])
        ring = sb("ring", [P, RING, 4096])
        hT = sb("hT", [P, KC, TOK])
        B = sb("B", [P, 4096])
        GB = sb("GB", [P, 2, D])
        MR = sb("MR", [P, 2, 512])
        rows = MR[:, 0, 0:384].rearrange("p (b d) -> p b d", b=3)
        WORK = sb("WORK", [P, 8704])
        small = sb("small", [P, 860])
        smalli = sb("smalli", [P, 48], U32)
        bank = [ctx.enter_context(nc.psum_tensor(f"bank{i}", [P, 512], F32)) for i in range(8)]
        h2d = nc.dram_tensor("h2_rows", (TOK, D), F32, kind="Internal").ap()
        yd = nc.dram_tensor("y_rows", (22 * ST, D), F32, kind="Internal").ap()

        def C(name, lo=0, hi=None):
            s, e = CONST[name]
            return cst[:, s + lo:(e if hi is None else s + hi)]

        ident = C("ident")
        used = [0]

        def cut(n):
            used[0] += n
            return small[:, used[0] - n:used[0]]

        ss = cut(4)
        rstd = cut(4)
        XS = B[:, :].rearrange("p (i d) -> p i d", i=NT)
        mixT = B[:, :].rearrange("p (m t) -> p m t", m=8)

        def slot(n, w=512):
            return ring[:, n % RING, 0:8 * w].rearrange("p (k n) -> p k n", k=8)

        def loaded(eng, n):
            eng.wait_ge(sem(f"weights_in{n % RING}"), 32 * (n // RING + 1))

        def passed(eng):
            eng.sem_inc(sem("passed"), 1)

        def load_sources(u):
            n = where[u]
            if u[0] == "mod":
                _, L, v, h = u
                c0 = v * D + h * 512
                src = a["mod_w"][L].rearrange("(k p) n -> p k n", p=P)
                s = slot(n)
                return [(s[:, :, 256 * i:256 * i + 256], src[:, :, c0 + 256 * i:c0 + 256 * i + 256]) for i in (0, 1)]
            if u[0] == "win":
                src = a["even_w_in"][0].rearrange("(k p) n -> p k n", p=P)
                s = slot(n)
                at = (256 * u[1], 512 + 256 * u[1]) if u[1] < 2 else (1024, 1280)
                return [(s[:, :, 256 * i:256 * i + 256], src[:, :, at[i]:at[i] + 256]) for i in (0, 1)]
            if u[0] == "wout":
                src = a["even_w_out" if u[1] == 0 else "odd_w_out"][0].rearrange("(k p) n -> p k n", p=P)
                s = slot(n)
                c0 = 512 * u[2]
                return [(s[:, :, 256 * i:256 * i + 256], src[:, :, c0 + 256 * i:c0 + 256 * i + 256]) for i in (0, 1)]
            if u[0] == "oin":
                lo, hi = OIN[u[1]]
                src = a["odd_w_in"][0].rearrange("(k p) n -> p k n", p=P)
                s = slot(n, hi - lo)
                return [(s[:, 4 * i:4 * i + 4, :], src[:, 4 * i:4 * i + 4, lo:hi]) for i in (0, 1)]
            if u[0] == "lora":
                flat = ring[:, n % RING, :]
                return [(flat[:, 0:1536].rearrange("p (k n) -> p k n", k=2),
                         a["mla_w_uq"][0].rearrange("(k p) n -> p k n", p=P)),
                        (flat[:, 1536:2560], a["mla_w_ukv"][0])]
            raise ValueError(u)

        def expert_sources(L, e, n, what):
            if what == "gu":
                s = slot(n)
                return [(s[:, :, 256 * i:256 * i + 256],
                         a[name][L, e].rearrange("(k p) n -> p k n", p=P)) for i, name in enumerate(("moe_w_gate", "moe_w_up"))]
            d = ring[:, n % RING, :].rearrange("p (x f n) -> p x f n", x=2, f=2)
            return [(d[:, i], a["moe_w_down"][L, e + i].rearrange("(f p) n -> p f n", p=P)) for i in (0, 1)]

        def routing(L):
            nt, c, over, ntile = moe_plan(L)
            base = used[0]

            r = {}
            for name, w in (("score", nt * 32), ("biased", nt * 32), ("hl", nt * 16 * 2), ("m12", nt * 8 * 3), ("gs", nt * 8),
                            ("gm", nt), ("G", nt * 8), ("sel4", nt * 8), ("w4", nt * 8), ("wsum", nt), ("winv", nt),
                            ("sc1", nt * 8), ("rank", nt), ("q", nt), ("m", nt), ("tile", nt), ("isov", nt), ("tmp", nt * 2), ("ov", 8),
                            ("excl", 8), ("posf", nt), ("gov", 8)):
                r[name] = cut(w)
            used[0] = base
            return r

        ITEMS = ([("kd", t, 0) for t in range(4)] + [("vd", t, 0) for t in range(4)] + [("ckv", t, 0) for t in range(4)]
                 + [("ql", t, 0) for t in (2, 3)] + [("qd", t, 0) for t in (2, 3)]
                 + [("qm", t, p) for t in (2, 3) for p in (0, 1)] + [("kvm", t, p) for t in range(4) for p in (0, 1)])
        UNITS = [(d, h, t) for d in (0, 1) for h in range(4) for t in range(2)]

        wk = WORK
        big = wk[:, 0:1024]
        onehot = wk[:, 1024:1536]
        brhs = wk[:, 1536:1536 + 4 * 110]
        cwt = wk[:, 2048:2048 + 44]
        XG = [wk[0:ST, 2112 + 1024 * i:3136 + 1024 * i] for i in (0, 1)]
        HG = [wk[:, 4160 + 512 * i:4672 + 512 * i].rearrange("p (k s) -> p k s", k=KC) for i in (0, 1)]
        SG = [wk[:, 5184 + 256 * i:5440 + 256 * i] for i in (0, 1)]
        T1 = [wk[:, 5696 + 256 * i:5952 + 256 * i] for i in (0, 1)]
        HE = [wk[:, 6208 + 256 * i:6464 + 256 * i] for i in (0, 1)]
        HET = [wk[:, 6720 + 256 * i:6976 + 256 * i].rearrange("p (f s) -> p f s", f=2) for i in (0, 1)]
        YO = [wk[:, 7232 + 512 * i:7744 + 512 * i] for i in (0, 1)]

        YP = wk[:, 0:2288].rearrange("p (m s t) -> p m s t", m=4, s=2)
        PP = wk[:, 2288:2288 + 2176].rearrange("p (g s t) -> p g s t", g=4, s=2)
        CV = wk[:, 4464:4464 + 2048].rearrange("p (m t) -> p m t", m=4)
        ACC = [wk[:, 6512 + 512 * i:7024 + 512 * i] for i in (0, 1)]
        SGL = [wk[:, 7536 + 512 * i:8048 + 512 * i] for i in (0, 1)]
        TA = GB[:, 0, 0:544].rearrange("p (s t) -> p s t", s=2)
        TB = GB[:, 1, 0:544].rearrange("p (s t) -> p s t", s=2)
        LNS = hT[:, 0:4, :]
        stats = cut(24)
        mv = cut(8)
        lrs = cut(4)

        class Chain:

            def __init__(self, eng, name):
                self.eng, self.s, self.n = eng, sem(name), 0

            def __call__(self, ins):
                self.n += 1
                ins.then_inc(self.s, 1)
                self.eng.wait_ge(self.s, self.n)

        block = ctx.enter_context(nc.Block())

        MOD_PAIRS = [u[1:3] for u in STREAM if u[0] == "mod" and u[3] == 0]

        def freed(n):
            u = STREAM[n]
            if u[0] == "mod":
                return "mod_mm", MOD_PAIRS.index(u[1:3]) + 1
            if u[0] == "win":
                return ("value_mm", 2 * u[1] + 2) if u[1] < 2 else ("pool_mm", 4)
            if u[0] == "wout":
                return "out_mm", 8 * u[1] + (u[2] + 1) * (4, 2)[u[1]]
            if u[0] == "oin":
                return "proj_mm", 1 + max(i for i, it in enumerate(ITEMS) if it[0] == ("kd", "vd", "ckv", "ql", "qd")[u[1]])
            if u[0] == "lora":
                return "proj_mm", len(ITEMS)
            if u[0] == "gu":
                return "gu_done", 16 * u[1] + u[2] // 2 + 1
            return "down_done", 16 * u[1] + u[2] + 1

        QN = [wk[:, 512 * i:512 * i + 512] for i in (0, 1)]
        SQ = [wk[:, 1024 + 512 * i:1536 + 512 * i] for i in (0, 1)]
        KR = wk[:, 2048:2304].rearrange("p (t d) -> p t d", t=4)
        kTr = wk[:, 2304:3328].rearrange("p (a t) -> p a t", a=2)
        qTn = wk[:, 3328:4352].rearrange("p (h t) -> p h t", h=4)
        qTr = wk[:, 4352:4864].rearrange("p (a t) -> p a t", a=2)
        qdT = wk[:, 4864:5888].rearrange("p (h t) -> p h t", h=4)
        cqT = wk[:, 5888:6400].rearrange("p (k t) -> p k t", k=2)
        ckvT = wk[:, 6400:6912]
        PT = [wk[:, 6912 + 512 * i:7424 + 512 * i] for i in (0, 1)]
        RA = wk[:, 6912:7424]
        OR = [wk[:, 7936 + 128 * i:8064 + 128 * i] for i in (0, 1)]
        RT = [wk[:, 8192 + 128 * i:8320 + 128 * i] for i in (0, 1)]
        kTn = hT[:, 0:4, :]
        VM = hT[:, 4:8, :]
        kdT = B[:, 0:2048].rearrange("p (h t) -> p h t", h=4)
        oT = B[:, 2048:4096].rearrange("p (c t) -> p c t", c=8)
        VD = X[:, 0:2, :].rearrange("p a (b d) -> p (a b) d", b=2)
        EX = GB[:, :, :].rearrange("p a (b d) -> p a b d", b=2)
        ssq = cut(8)
        rs = cut(16)
        ssr = cut(4)
        mx = cut(4)
        nb = cut(4)
        es = cut(4)
        ri = cut(4)
        oss = cut(2)
        ors = cut(2)
        lam = cut(8)
        subs = cut(1)
        lamp = OR[0]
        OUTT = [wk[:, 6512 + 512 * i:7024 + 512 * i] for i in (0, 1)]

        def count(i, kinds):
            return sum(it[0] in kinds for it in ITEMS[:i])

        NORMED = ("kd", "ckv", "ql", "qd", "qm", "kvm")
        BLOCKS = {"kd": 4, "qd": 4, "ckv": 1, "ql": 2, "qm": 3, "kvm": 3}

        def project_pe(pe, turn_x, loaded):

            def source(i):
                kind, t, p = ITEMS[i]
                if i >= 2:
                    pe.wait_ge(sem("item_act"), i - 1)
                    if count(i - 1, NORMED):
                        pe.wait_ge(sem("item_dve"), count(i - 1, NORMED))
                dst = bank[i % 2]
                if kind in ("kd", "vd", "ckv", "ql", "qd"):
                    j = ("kd", "vd", "ckv", "ql", "qd").index(kind)
                    lo, hi = OIN[j]
                    n = where[("oin", j)]
                    if t == (2 if kind in ("ql", "qd") else 0):
                        loaded(pe, n)
                    w = slot(n, hi - lo)
                    for k in range(KC):
                        mm = pe.matmul(dst[:, 0:hi - lo], hT[:, k, t * P:(t + 1) * P], w[:, k, :], start=k == 0, stop=k == KC - 1)
                else:
                    n = where[("lora",)]
                    flat = ring[:, n % RING, :]
                    if i == count(99, NORMED[:4]) + 4:
                        loaded(pe, n)
                        pe.wait_ge(sem("cols"), count(i, NORMED))
                    if kind == "qm":
                        for k in range(2):
                            mm = pe.matmul(dst[:, 0:384], cqT[:, k, (t - 2) * P:(t - 1) * P],
                                           flat[:, 768 * k + 384 * p:768 * k + 384 * p + 384], start=k == 0, stop=k == 1)
                    else:
                        mm = pe.matmul(dst[:, :], ckvT[:, t * P:(t + 1) * P], flat[:, 1536 + 512 * p:2048 + 512 * p],
                                       start=True, stop=True)
                mm.then_inc(sem("proj_mm"), 1)

            def turn(i):
                kind, t, p = ITEMS[i]
                if kind == "vd":
                    return
                c = count(i, NORMED)
                if c >= 2:
                    pe.wait_ge(sem("cols"), c - 1)
                pe.wait_ge(sem("rows_done"), c + 1)
                for b in range(BLOCKS[kind]):
                    src = QN[c % 2][:, b * P:(b + 1) * P]
                    if kind == "qm":
                        src = QN[c % 2][:, 192 * b:192 * b + P] if b < 2 else RT[c % 2]
                    if kind == "kvm" and b == 2:
                        src = RT[c % 2]
                    mm = pe.transpose(bank[2 + c % 2][:, b * P:(b + 1) * P], src, ident)
                mm.then_inc(sem("cols_turned"), 1)

            for i in range(len(ITEMS)):
                if ITEMS[i][0] == "qm" and ITEMS[i - 1][0] == "qd":
                    turn(i - 1)
                    source(i)
                    continue
                source(i)
                if i:
                    if not (ITEMS[i - 1][0] == "qd" and ITEMS[i][0] == "qm"):
                        turn(i - 1)
            turn(len(ITEMS) - 1)

        def attention_pe(pe):
            pe.wait_ge(sem("cols"), count(99, NORMED))
            n_units = len(UNITS)

            def scores(i):
                d, h, t = UNITS[i]
                if i >= 2:
                    pe.wait_ge(sem("exp_done"), i - 1)
                b0 = bank[2 * (i % 2)]
                q = slice(t * P, (t + 1) * P)
                if not d:
                    r = 64 * (h % 2)
                    pe.matmul(b0[:, :], qTn[:, h, q], kTn[:, h, :], start=True, stop=False)
                    mm = pe.matmul(b0[:, :], qTr[r:r + 64, h // 2, q], kTr[r:r + 64, h // 2, :], start=False, stop=True)
                else:
                    for m in range(2):
                        mm = pe.matmul(bank[2 * (i % 2) + m][:, :], qdT[64 * m:64 * m + 64, h, q], kdT[64 * m:64 * m + 64, h, :],
                                       start=True, stop=True)
                mm.then_inc(sem("score_mm"), 1)

            def probs(i):
                pe.wait_ge(sem("probs_ready"), i + 1)
                if i:
                    pe.wait_ge(sem("pt_done"), i)
                for c in range(4):
                    mm = pe.transpose(bank[4][:, c * P:(c + 1) * P], EX[:, i % 2, 0, c * P:(c + 1) * P], ident)
                mm.then_inc(sem("probs_turned"), 1)

            def values(i):
                d, h, t = UNITS[i]
                pe.wait_ge(sem("pt_done"), i + 1)
                if i:
                    pe.wait_ge(sem("o_rows"), i)
                v = VD if d else VM
                for c in range(4):
                    mm = pe.matmul(bank[5][:, 0:P], PT[i % 2][:, c * P:(c + 1) * P], v[:, c, h * P:(h + 1) * P], start=c == 0, stop=c == 3)
                mm.then_inc(sem("pv_mm"), 1)

            def turn_o(i):
                pe.wait_ge(sem("o_rows"), i + 1)
                if i:
                    pe.wait_ge(sem("o_cols"), i)
                pe.transpose(bank[6][:, 0:P], OR[i % 2], ident).then_inc(sem("o_turned"), 1)

            for i in range(n_units + 2):
                if i < n_units:
                    scores(i)
                if 0 <= i - 2:
                    turn_o(i - 2)
                if 0 <= i - 1 < n_units:
                    probs(i - 1)
                    values(i - 1)

        def attention_scalar(act):
            def cols(i):
                kind, t, p = ITEMS[i]
                if kind == "vd":
                    return
                c = count(i, NORMED)
                act.wait_ge(sem("cols_turned"), c + 1)
                src = bank[2 + c % 2]
                tk, tq = slice(t * P, (t + 1) * P), slice((t - 2) * P, (t - 1) * P)
                four = src[:, :].rearrange("p (h t) -> p h t", h=4)
                if kind == "kd":
                    ins = act.activation(kdT[:, :, tk], four, ACT.Copy)
                elif kind == "qd":
                    ins = act.activation(qdT[:, :, tq], four, ACT.Copy)
                elif kind == "ckv":
                    ins = act.activation(ckvT[:, tk], src[:, 0:P], ACT.Identity, scale=par[:, R_GCKV:R_GCKV + 1])
                elif kind == "ql":
                    for k in range(2):
                        ins = act.activation(cqT[:, k, tq], src[:, k * P:(k + 1) * P], ACT.Identity, scale=par[:, R_GCQ + k:R_GCQ + k + 1])
                elif kind == "qm":
                    act.activation(qTn[:, 2 * p:2 * p + 2, tq], four[:, 0:2, :], ACT.Identity, scale=par[:, R_QN:R_QN + 1])
                    ins = act.activation(qTr[:, p, tq], four[:, 2, :], ACT.Copy)
                else:
                    act.activation(kTn[:, 2 * p:2 * p + 2, tk], four[:, 0:2, :], ACT.Identity, scale=par[:, R_KN:R_KN + 1])
                    ins = act.activation(kTr[:, p, tk], four[:, 2, :], ACT.Copy)
                ins.then_inc(sem("cols"), 1)

            for i, (kind, t, p) in enumerate(ITEMS):
                early = kind == "qm" and ITEMS[i - 1][0] == "qd"
                if early:
                    cols(i - 1)
                act.wait_ge(sem("proj_mm"), i + 1)
                src = bank[i % 2]
                c = count(i, NORMED)
                if kind != "vd" and c >= 2:
                    act.wait_ge(sem("rows_done"), c - 1)
                if kind == "vd":
                    act.wait_ge(sem("xs"), 12)
                    ins = act.activation(VD[:, t, :], src[:, :], ACT.Copy)
                elif kind == "kvm":
                    two = src[:, :].rearrange("p (h d) -> p h d", h=2)
                    act.activation(VM[:, t, 256 * p:256 * p + 256].rearrange("p (h d) -> p h d", h=2), two[:, :, P:2 * P], ACT.Copy)
                    ins = act.activation(SQ[c % 2][:, 0:256].rearrange("p (h d) -> p h d", h=2), two[:, :, 0:P], ACT.Square)
                else:
                    w = {"kd": 512, "qd": 512, "ckv": 192, "ql": 256, "qm": 384}[kind]
                    ins = act.activation(SQ[c % 2][:, 0:w], src[:, 0:w], ACT.Square)
                ins.then_inc(sem("item_act"), 1)
                if i and not early:
                    cols(i - 1)
            cols(len(ITEMS) - 1)
            act.wait_ge(sem("lam_dots"), 1)
            act.wait_ge(sem("sub_scale"), 1)
            act.activation(lam[:, 2:4], lam[:, 0:2], ACT.Exp).then_inc(sem("lam_exp"), 1)
            n_units = len(UNITS)

            def exps(i):
                d = UNITS[i][0]
                act.wait_ge(sem("max_done"), i + 1)
                if i >= 2:
                    act.wait_ge(sem("probs_turned"), i - 1)
                for m in range(1 + d):
                    ins = act.activation(EX[:, i % 2, m, :], bank[2 * (i % 2) + m][:, :], ACT.Exp, bias=nb[:, 2 * (i % 2) + m:2 * (i % 2) + m + 1],
                                         scale=(MLA_SCALE, DIFF_SCALE)[d], accum_out=es[:, 2 * (i % 2) + m:2 * (i % 2) + m + 1])
                ins.then_inc(sem("exp_done"), 1)

            def o_cols(i):
                d, h, t = UNITS[i]
                act.wait_ge(sem("o_turned"), i + 1)
                scale = subs[:, 0:1] if d else 1.0
                act.activation(oT[:, 4 * d + h, t * P:(t + 1) * P], bank[6][:, 0:P], ACT.Identity, scale=scale).then_inc(sem("o_cols"), 1)

            for i in range(n_units + 2):
                if i < n_units:
                    exps(i)
                if 0 <= i - 2:
                    o_cols(i - 2)
                if 0 <= i - 1 < n_units:
                    act.wait_ge(sem("probs_turned"), i)
                    if i - 1 >= 2:
                        act.wait_ge(sem("pv_mm"), i - 2)
                    act.activation(PT[(i - 1) % 2], bank[4][:, :], ACT.Copy).then_inc(sem("pt_done"), 1)
                    if UNITS[i - 1][0]:
                        j = (i - 1) % 2
                        act.wait_ge(sem("pv_mm"), i)
                        if i - 1 >= 2:
                            act.wait_ge(sem("o_rows"), i - 2)
                        act.activation(OR[j], bank[5][:, 0:P], ACT.Square, accum_out=oss[:, j:j + 1]).then_inc(sem("o_squares"), 1)

        def moe_scalar(act, L, gate_rows, experts):
            nt, c, over, ntile = moe_plan(L)
            act.wait_ge(sem("logit_parts"), L + 1)
            act.activation(MR[:, 0, 0:nt * P], bank[6][:, 0:nt * P], ACT.Copy).then_inc(sem("logit_rows"), 1)
            act.wait_ge(sem("logits"), L + 1)
            act.activation(routing(L)["score"], bank[2][:, 0:nt * 32], ACT.Sigmoid).then_inc(sem("scored"), 1)
            for i in range(2 * nt):
                act.wait_ge(sem("h2_turned"), 8 * L + i + 1)
                act.activation(B[:, 512 * i:512 * i + 512], bank[3 + i % 2][:, :], ACT.Copy).then_inc(sem("h2_rows"), 1)
            gate_rows(f"m{L}", (0, 1) if L == 0 else (1,))
            experts(L)
            overflow_scalar(act, L)

        def group_loop(eng, L, body, skipped):
            c = moe_plan(L)[1]
            with eng.Fori(0, GROUPS) as g:
                if c == 1:
                    body(g, (0,), None)
                else:
                    two = eng.value_load(smalli[0:1, bass.ds(g + 40, 1)], min_val=0, max_val=1)
                    with eng.If(two > 0):
                        body(g, (0, 1), None)
                    with eng.Else():
                        body(g, (0,), skipped)

        def expert_slot_freed(eng, L, done, v):
            for s in range(moe_plan(L)[1]):
                eng.wait_ge(sem(f"{done}_{s}"), v)

        def bump(eng, names):
            for name, n in names:
                eng.sem_inc(sem(name), n)

        def overflow_count(eng, L):
            eng.wait_ge(sem("slots_ready"), L + 1)
            return eng.value_load(smalli[0:1, 33:34], min_val=0, max_val=moe_plan(L)[2])

        gu_over = hT[:, :, :]
        dn_over = B[:, :].rearrange("p (x f n) -> p x f n", x=2, f=2)

        def overflow_scalar(act, L):
            n = overflow_count(act, L)
            with act.If(n > 0):
                act.sem_inc(sem(f"over_rows{L}"), 1)
                with act.Fori(0, n) as j:
                    for q in range(2):
                        act.wait_ge(sem(f"over_gu{L}"), 4 * j + 2 * q + 3)
                        act.activation(SG[0], bank[1][:, 0:DE], ACT.Sigmoid).then_inc(sem(f"over_sg{L}"), 1)
                        act.wait_ge(sem(f"over_he_turned{L}"), 2 * j + q + 1)
                        act.activation(HET[0].rearrange("p f s -> p (f s)"), bank[3][:, 0:DE], ACT.Copy).then_inc(sem(f"over_het{L}"), 1)
                    act.wait_ge(sem(f"over_down{L}"), 2 * j + 3)
                    act.activation(YO[0], bank[5][:, :], ACT.Copy).then_inc(sem(f"over_rows{L}"), 1)
            with act.Else():
                act.nop()
            act.nop()

        def overflow_pe(pe, L):
            n = overflow_count(pe, L)
            with pe.If(n > 0):
                for name in ("over_gu", "over_down"):
                    pe.sem_inc(sem(f"{name}{L}"), 1)
                with pe.Fori(0, n) as j:
                    pe.wait_ge(sem(f"over_gathered{L}"), 16 * j + 16)
                    passed(pe)
                    for k in range(KC):
                        mm = pe.transpose(bank[0][:, k * ST:(k + 1) * ST], XG[0][:, k * P:(k + 1) * P], ident[0:ST, 0:ST])
                    mm.then_inc(sem(f"over_turned{L}"), 1)
                    pe.wait_ge(sem(f"over_hg{L}"), j + 1)
                    for q in range(2):
                        pe.wait_ge(sem(f"over_he{L}"), 2 * j + q + 1)
                        for x in range(2):
                            pe.wait_ge(sem(f"over_gu_in{L}"), 128 * j + 64 * q + 32 * x + 32)
                            for k in range(KC):
                                mm = pe.matmul(bank[1][ST * x:ST * x + ST, :], HG[0][:, k, :], gu_over[:, k, :], start=k == 0, stop=k == KC - 1)
                            mm.then_inc(sem(f"over_gu{L}"), 1)
                        pe.wait_ge(sem(f"over_he{L}"), 2 * j + q + 2)
                        for f in range(2):
                            mm = pe.transpose(bank[3][:, f * P:(f + 1) * P], HE[0][:, f * P:(f + 1) * P], ident)
                        mm.then_inc(sem(f"over_he_turned{L}"), 1)
                        pe.wait_ge(sem(f"over_het{L}"), 2 * j + q + 1)
                        pe.wait_ge(sem(f"over_down_in{L}"), 64 * j + 32 * q + 32)
                        if q == 0:
                            pe.wait_ge(sem(f"over_rows{L}"), j + 1)
                        for f in range(2):
                            for x in range(2):
                                for h in range(2):
                                    mm = pe.matmul(bank[5][ST * h:ST * h + ST, :], HET[0][:, f, ST * x:ST * x + ST],
                                                   dn_over[:, x, f, 512 * h:512 * h + 512],
                                                   start=q == 0 and f == 0 and x == 0, stop=q == 1 and f == 1 and x == 1)
                        mm.then_inc(sem(f"over_down{L}"), 1)
            with pe.Else():
                pe.nop()
            pe.nop()

        def overflow_vector(dve, L):
            c = moe_plan(L)[1]
            n = overflow_count(dve, L)
            with dve.If(n > 0):
                dve.sem_inc(sem(f"over_he{L}"), 1)
                with dve.Fori(0, n) as j:
                    dve.wait_ge(sem(f"over_turned{L}"), j + 1)
                    dve.tensor_copy(HG[0].rearrange("p k s -> p (k s)"), bank[0][:, :]).then_inc(sem(f"over_hg{L}"), 1)
                    for q in range(2):
                        dve.wait_ge(sem(f"over_sg{L}"), 2 * j + q + 1)
                        dve.scalar_tensor_tensor(out=T1[0], in0=SG[0], scalar=cwt[:, bass.ds(2 * j + (16 * c + q), 1)],
                                                 in1=bank[1][:, 0:DE], op0=ALU.mult, op1=ALU.mult).then_inc(sem(f"over_t1{L}"), 1)
                        dve.wait_ge(sem(f"over_t1{L}"), 2 * j + q + 1)
                        dve.tensor_tensor(HE[0], T1[0], bank[1][:, DE:2 * DE], ALU.mult).then_inc(sem(f"over_he{L}"), 1)
            with dve.Else():
                dve.nop()
            dve.nop()

        def overflow_pool(pool, L):
            c = moe_plan(L)[1]
            n = overflow_count(pool, L)
            with pool.If(n > 0):
                with pool.Fori(0, n) as j:
                    pool.tensor_copy(smalli[0:ST, 34:35], smalli[0:ST, bass.ds(j + (4 + 8 * c), 1)]).then_inc(sem(f"over_index{L}"), 1)
                    pool.wait_ge(sem(f"over_index{L}"), j + 1)
                    passed(pool)
                    pool.indirect_dma_start(XG[0], None, h2d[:, :], bass.IndirectOffsetOnAxis(ap=smalli[0:ST, 34:35], axis=0))\
                        .then_inc(sem(f"over_gathered{L}"), 16)
                    grp = pool.value_load(smalli[0:1, bass.ds(j + 26, 1)], min_val=0, max_val=GROUPS - 1)
                    for q in range(2):
                        for x in range(2):
                            pool.wait_ge(sem(f"over_gu{L}"), 4 * j + 2 * q + x + 1)
                            passed(pool)
                            for i, name in enumerate(("moe_w_gate", "moe_w_up")):
                                pool.dma_start(gu_over[:, :, 256 * i:256 * i + 256],
                                               a[name][L, grp * EPG + 2 * q + x].rearrange("(k p) n -> p k n", p=P)).then_inc(sem(f"over_gu_in{L}"), 16)
                        pool.wait_ge(sem(f"over_down{L}"), 2 * j + q + 1)
                        passed(pool)
                        for x in range(2):
                            pool.dma_start(dn_over[:, x], a["moe_w_down"][L, grp * EPG + 2 * q + x].rearrange("(f p) n -> p f n", p=P))\
                                .then_inc(sem(f"over_down_in{L}"), 16)
                    pool.wait_ge(sem(f"over_rows{L}"), j + 2)
                    passed(pool)
                    for h in range(2):
                        pool.dma_start(yd[bass.ds(j * ST + 8 * c * ST, ST), 512 * h:512 * h + 512], YO[0][ST * h:ST * h + ST, :])\
                            .then_inc(sem(f"over_stored{L}"), 16)
                    pool.wait_ge(sem(f"over_stored{L}"), 32 * j + 32)
            with pool.Else():
                pool.nop()
            pool.nop()

        def nth(tag):
            return ("a0", "m0", "a1", "m1").index(tag)

        def gates_before(tag):
            return {"a0": 0, "m0": 4, "a1": 8, "m1": 10}[tag]

        def x_tiles(tag):
            return (2, 3) if tag == "m1" else (0, 1, 2, 3)

        def norm_of(tag):
            return int(tag[1]), int(tag[0] == "m"), 3 * int(tag[0] == "m")

        def stream_cols(tag):
            return [(1, 0, 256)] if tag == "m1" else [(0, 0, 256), (1, 256, 512)]

        @block.sync
        def _(sp):
            def load(n, pairs):
                if n >= RING:
                    s, v = freed(n - RING)
                    if s in ("gu_done", "down_done"):
                        expert_slot_freed(sp, STREAM[n - RING][1], s, v)
                    else:
                        sp.wait_ge(sem(s), v)
                for dst, src in pairs:
                    sp.dma_start(dst, src).then_inc(sem(f"weights_in{n % RING}"), 16)

            for n, u in enumerate(STREAM):
                if n == 1:
                    sp.wait_ge(sem("rows_in"), 16 * 14)
                if n == 2:
                    xs = a["ctx"][0].rearrange("(i p) d -> i p d", p=P), a["x"][0].rearrange("(i p) d -> i p d", p=P)
                    for t in range(NT):
                        sp.dma_start(X[:, t, :], xs[t // 2][t % 2]).then_inc(sem("x_in"), 16)
                if u[0] not in ("gu", "down"):
                    load(n, load_sources(u))
                elif n < MOE_AT[u[1]] + RING:
                    load(n, expert_sources(u[1], u[2] * (2 if u[0] == "down" else 1), n, u[0]))
                elif n == MOE_AT[u[1]] + RING:
                    L = u[1]
                    m0 = MOE_AT[L]
                    with sp.Fori(1, GROUPS) as g:
                        for j in range(RING):
                            q, kind = j // 3, ("gu", "gu", "down")[j % 3]
                            done = "down_done" if kind == "down" else "gu_done"
                            expert_slot_freed(sp, L, done, 16 * L + 2 * g + (q - 1))
                            e = g * EPG + 2 * q + (j % 3 if kind == "gu" else 0)
                            for dst, src in expert_sources(L, e, m0 + j, kind):
                                sp.dma_start(dst, src).then_inc(sem(f"weights_in{(m0 + j) % RING}"), 16)

        @block.tensor
        def _(pe):
            pe.wait_ge(sem("rows_in"), 16 * 14)
            pe.wait_ge(sem("const_in"), 16)
            pe.transpose(bank[7][:, 0:128], rows[:, 0, :], ident)
            pe.transpose(bank[7][:, 128:252], rows[0:124, 1, :], ident[0:124, 0:124])
            pe.transpose(bank[7][:, 256:294], rows[0:NROWS3, 2, :], ident[0:NROWS3, 0:NROWS3]).then_inc(sem("par_turned"), 1)
            pe.wait_ge(sem("cs_ready"), 1)

            def mod_multiply(i):
                L, v = MOD_PAIRS[i]
                units = [where[("mod", L, v, h)] for h in (0, 1)]
                for n in units:
                    loaded(pe, n)
                if i:
                    pe.wait_ge(sem("mod_rows"), i)
                for k in range(KC):
                    for h in (0, 1):
                        at = 64 * h + 32 * (k % 2)
                        mm = pe.matmul(bank[6][at:at + 32, :], cs[:, k, :], slot(units[h])[:, k, :], start=k < 2, stop=k >= KC - 2)
                mm.then_inc(sem("mod_mm"), 1)

            def mod_turn(i):
                pe.wait_ge(sem("mod_rows"), i + 1)
                if i:
                    pe.wait_ge(sem("mod_cols"), i)
                for c in range(4):
                    mm = pe.matmul(bank[7][:, 4 * c:4 * c + 4], MR[:, i % 2, c * P:(c + 1) * P], C("sel"), start=True, stop=True)
                mm.then_inc(sem("mod_turned"), 1)

            def mod(i):
                mod_multiply(i)
                mod_turn(i)

            def turn_x(tag, tiles):
                w = len(tiles)
                pe.wait_ge(sem("xs"), 4 * nth(tag) + w)
                for k in range(KC):
                    if k >= 2:
                        pe.wait_ge(sem(f"ht_{k % 2}"), 4 * nth(tag) + k // 2)
                    for j, t in enumerate(tiles):
                        mm = pe.transpose(bank[k % 2][:, j * P:(j + 1) * P], XS[:, t, k * P:(k + 1) * P], ident)
                    mm.then_inc(sem("turned"), 1)

            def gates(tag, L, v, streams):
                n = 0
                for s in streams:
                    for h in range(2):
                        if n >= 2:
                            pe.wait_ge(sem("gate_rows"), gates_before(tag) + n - 1)
                        for c in range(4):
                            mm = pe.matmul(bank[4 + n % 2][:, c * P:(c + 1) * P],
                                           mods[:, L, v, 4 * h + c, s:s + 1].to_broadcast([P, P]), ident, start=True, stop=True)
                        mm.then_inc(sem("gate_mms"), 1)
                        n += 1

            def project_out(L, lhs, tiles, between=None):
                for h in range(2):
                    n = where[("wout", L, h)]
                    w = slot(n)
                    loaded(pe, n)
                    for j, t in enumerate(tiles):
                        i = h * len(tiles) + j
                        if i >= 2:
                            pe.wait_ge(sem("out_used"), 8 * L + i - 1)
                        for k in range(KC):
                            mm = pe.matmul(bank[i % 2][:, :], lhs(k, j), w[:, k, :], start=k == 0, stop=k == KC - 1)
                        mm.then_inc(sem("out_mm"), 1)
                        if between:
                            between(i)

            def route(L):
                nt, c, over, ntile = moe_plan(L)
                for i in range(2):
                    pe.wait_ge(sem(f"ht_{i}"), 4 * nth(f"m{L}") + 4)
                pe.wait_ge(sem("router_in"), 16)
                for k in range(KC):
                    mm = pe.matmul(bank[6][32 * (k % 4):32 * (k % 4) + 32, 0:nt * P], rw[:, k, :], hT[:, k, 0:nt * P], start=k < 4, stop=k >= 4)
                mm.then_inc(sem("logit_parts"), 1)
                pe.wait_ge(sem("logit_rows"), L + 1)
                for t in range(nt):
                    mm = pe.matmul(bank[2][:, t * 32:t * 32 + 32], MR[:, 0, t * P:(t + 1) * P], C("sel32"), start=True, stop=True)
                mm.then_inc(sem("logits"), 1)
                for t in range(nt):
                    for h in range(2):
                        i = 2 * t + h
                        if i >= 2:
                            pe.wait_ge(sem("h2_rows"), 8 * L + i - 1)
                        for k in range(4):
                            mm = pe.transpose(bank[3 + i % 2][:, k * P:(k + 1) * P], hT[:, 4 * h + k, t * P:(t + 1) * P], ident)
                        mm.then_inc(sem("h2_turned"), 1)
                pe.wait_ge(sem("groups"), L + 1)
                G = routing(L)["G"]
                for t in range(nt):
                    for s in range(t + 1):
                        mm = pe.matmul(bank[5][:, 8 * t:8 * t + 8], C("lower") if s == t else C("ones"),
                                       G[:, 8 * s:8 * s + 8], start=s == 0, stop=s == t)
                for s in range(nt):
                    mm = pe.matmul(bank[5][:, 64:72], C("ones"), G[:, 8 * s:8 * s + 8], start=s == 0, stop=s == nt - 1)
                mm.then_inc(sem("ranks"), 1)
                pe.wait_ge(sem("onehot"), L + 1)
                for t in range(nt):
                    mm = pe.matmul(bank[6][:, 0:5 * ntile], onehot[:, t * P:(t + 1) * P],
                                   brhs[:, t * 5 * ntile:(t + 1) * 5 * ntile], start=t == 0, stop=t == nt - 1)
                mm.then_inc(sem("slots"), 1)
                pe.wait_ge(sem("h2_rows"), 8 * L + 2 * nt)

            def experts(L):
                nt, c, over, ntile = moe_plan(L)
                m0 = MOE_AT[L]
                pe.wait_ge(sem("slots_ready"), L + 1)

                def body(g, tiles, skipped):
                    for s in tiles:
                        pe.wait_ge(sem(f"gathered_{s}"), 128 * L + 16 * g + 16)
                        if s:
                            pe.wait_ge(sem(f"hg_{s - 1}"), 8 * L + g + 1)
                        passed(pe)
                        for k in range(KC):
                            mm = pe.transpose(bank[0][:, k * ST:(k + 1) * ST], XG[s][:, k * P:(k + 1) * P], ident[0:ST, 0:ST])
                        mm.then_inc(sem(f"hg_turned_{s}"), 1)
                    for q in range(2):
                        for s in tiles:
                            if q == 0:
                                pe.wait_ge(sem(f"hg_{s}"), 8 * L + g + 1)
                            if s == 0:
                                for x in range(2):
                                    n = m0 + 3 * q + x
                                    pe.wait_ge(sem(f"weights_in{n % RING}"), 32 * g + 32 * (n // RING + 1))
                            pe.wait_ge(sem(f"he_{s}"), 16 * L + 2 * g + q + 1)
                            for k in range(KC):
                                for x in range(2):
                                    mm = pe.matmul(bank[1 + s][ST * x:ST * x + ST, :], HG[s][:, k, :],
                                                   slot(m0 + 3 * q + x)[:, k, :], start=k == 0, stop=k == KC - 1)
                            mm.then_inc(sem(f"gu_done_{s}"), 1)
                        n = m0 + 3 * q + 2
                        pe.wait_ge(sem(f"weights_in{n % RING}"), 32 * g + 32 * (n // RING + 1))
                        dn = ring[:, n % RING, :].rearrange("p (x f n) -> p x f n", x=2, f=2)
                        for s in tiles:
                            pe.wait_ge(sem(f"he_{s}"), 16 * L + 2 * g + q + 2)
                            if skipped and q == 0:
                                bump(pe, skipped)
                            for f in range(2):
                                mm = pe.transpose(bank[3 + s][:, f * P:(f + 1) * P], HE[s][:, f * P:(f + 1) * P], ident)
                            mm.then_inc(sem(f"he_turned_{s}"), 1)
                        for s in tiles:
                            pe.wait_ge(sem(f"het_{s}"), 16 * L + 2 * g + q + 1)
                            if q == 0:
                                pe.wait_ge(sem(f"y_rows_{s}"), 8 * L + g + 1)
                            for f in range(2):
                                for x in range(2):
                                    for h in range(2):
                                        mm = pe.matmul(bank[5 + s][ST * h:ST * h + ST, :], HET[s][:, f, ST * x:ST * x + ST],
                                                       dn[:, x, f, 512 * h:512 * h + 512],
                                                       start=q == 0 and f == 0 and x == 0, stop=q == 1 and f == 1 and x == 1)
                            mm.then_inc(sem(f"down_done_{s}"), 1)

                group_loop(pe, L, body, [("hg_turned_1", 1), ("gu_done_1", 2), ("he_turned_1", 2), ("down_done_1", 2)])

            for i in range(2):
                mod(i)
            turn_x("a0", range(4))
            for i in range(2):
                pe.wait_ge(sem(f"ht_{i}"), 4)
            for m in range(4):
                n = where[("win", m // 2)]
                w = slot(n)
                loaded(pe, n)
                for part in (1, 0):
                    b = bank[2 * (m % 2) + part]
                    if m >= 2:
                        pe.wait_ge(sem("glu_done"), m - 1)
                    for k in range(KC):
                        mm = pe.matmul(b[:, :], w[:, k, 256 * part + P * (m % 2):256 * part + P * (m % 2) + P], hT[:, k, :],
                                       start=k == 0, stop=k == KC - 1)
                    mm.then_inc(sem("value_mm" if part == 0 else "gate_mm"), 1)
            n = where[("win", 2)]
            w = slot(n)
            loaded(pe, n)
            for g in range(4):
                if g >= 2:
                    pe.wait_ge(sem("pool_in"), g - 1)
                for k in range(KC):
                    mm = pe.matmul(bank[4 + g % 2][:, :], w[:, k, P * g:P * g + P], hT[:, k, :], start=k == 0, stop=k == KC - 1)
                mm.then_inc(sem("pool_mm"), 1)
            for i in range(2, 6):
                mod(i)
            pe.wait_ge(sem("pool_w_in"), 16)
            pe.wait_ge(sem("pooled"), 4)
            for g in range(4):
                if g == 0:
                    pe.wait_ge(sem("pool_in"), 4)
                if g >= 2:
                    pe.wait_ge(sem("pool_out"), g - 1)
                pe.matmul(bank[4 + g % 2][:, :], pw[:, g, :], mixT[:, g, :], start=True, stop=True).then_inc(sem("pool_mix"), 1)
            pe.wait_ge(sem("conv_done"), 4)
            for t in range(NT):
                if t == 0:
                    pe.wait_ge(sem("glu_done"), 4)
                for m in range(4):
                    mm = pe.transpose(bank[t][:, m * P:(m + 1) * P], CV[:, m, t * P:(t + 1) * P], ident)
                mm.then_inc(sem("conv_turned"), 1)
            pe.wait_ge(sem("mod_cols"), 6)
            pe.wait_ge(sem("pool_out"), 4)
            gates("a0", 0, 2, (0, 1))
            for m in range(4):
                if m == 0:
                    pe.wait_ge(sem("ln_rows"), 4)
                for t in range(NT):
                    mm = pe.transpose(bank[m][:, t * P:(t + 1) * P], LNS[:, t, m * P:(m + 1) * P], ident)
                mm.then_inc(sem("ln_turned"), 1)
            pe.wait_ge(sem("mix_done"), 4)

            def layer1_mods(i):
                if i % 2 == 1:
                    mod_multiply(6 + i // 2)
                elif i:
                    mod_turn(5 + i // 2)

            project_out(0, lambda k, j: mixT[:, k, j * P:(j + 1) * P], range(4), layer1_mods)
            mod_turn(9)
            for i in range(10, 12):
                mod(i)
            turn_x("m0", range(4))
            route(0)
            gates("m0", 0, 5, (0, 1))
            experts(0)
            overflow_pe(pe, 0)
            turn_x("a1", range(4))
            for i in range(2):
                pe.wait_ge(sem(f"ht_{i}"), 12)
            project_pe(pe, turn_x, loaded)
            attention_pe(pe)
            gates("a1", 1, 2, (1,))
            pe.wait_ge(sem("o_cols"), len(UNITS))
            project_out(1, lambda k, j: oT[:, k, j * P:(j + 1) * P], (2, 3))
            turn_x("m1", (2, 3))
            route(1)
            gates("m1", 1, 5, (1,))
            experts(1)
            overflow_pe(pe, 1)

        @block.scalar
        def _(act):
            r1 = "(o p) -> o p"
            act.dma_start(rows[96:128, 0, :], a["norm_g"].rearrange("i n (c p) -> (i n c) p", p=P)).then_inc(sem("rows_in"), 16)
            act.dma_start(rows[0:96, 0, :], a["mod_b"].rearrange("i (v p) -> (i v) p", p=P)).then_inc(sem("rows_in"), 16)
            act.dma_start(rows[0:124, 1, :], a["conv_dw_w"][0].rearrange("t (c p) -> (t c) p", p=P)).then_inc(sem("rows_in"), 16)
            for r, n, src in ((R_CCTX, 8, a["c_ctx"].rearrange(r1, p=P)), (R_C, 8, a["c"][0].rearrange(r1, p=P)),
                              (R_DWB, 4, a["conv_dw_b"][0].rearrange(r1, p=P)), (R_LNG, 4, a["conv_ln_g"][0].rearrange(r1, p=P)),
                              (R_LNB, 4, a["conv_ln_b"][0].rearrange(r1, p=P)), (R_PSC, 4, a["pool_scale"][0].rearrange(r1, p=P)),
                              (R_GCQ, 2, a["mla_g_cq"][0].rearrange(r1, p=P)), (R_GCKV, 1, a["mla_g_ckv"]),
                              (R_SUBG, 1, a["diff_sub_g"]), (R_QN, 1, a["qk_g_mla"][0, 0:1, 0:P]), (R_KN, 1, a["qk_g_mla"][0, 1:2, 0:P])):
                act.dma_start(rows[r - 256:r - 256 + n, 2, :], src).then_inc(sem("rows_in"), 16)

            for s in range(2):
                act.sem_inc(sem(f"y_rows_{s}"), 1)

            act.wait_ge(sem("par_ready"), 1)
            act.activation(csg[:, :], par[:, R_CCTX:R_CCTX + 16], ACT.Sigmoid).then_inc(sem("cs_sig"), 1)

            def square_rows(tag):
                if tag == "a0":
                    act.wait_ge(sem("x_in"), 64)
                else:
                    act.wait_ge(sem(f"x_done_{tag}"), 1)
                for t in x_tiles(tag):
                    if tag == "a1" and t:
                        act.wait_ge(sem("x_done_a1"), t + 1)
                    act.activation(hT[:, 2 * t:2 * t + 2, :].rearrange("p k t -> p (k t)"), X[:, t, :], ACT.Square,
                                   accum_out=ss[:, t:t + 1]).then_inc(sem("ss"), 1)

            def mod_rows(i):
                act.wait_ge(sem("mod_mm"), i + 1)
                act.activation(MR[:, i % 2, :], bank[6][:, :], ACT.Copy).then_inc(sem("mod_rows"), 1)
                L, v = MOD_PAIRS[i]
                act.wait_ge(sem("mod_turned"), i + 1)
                for k in range(KC):
                    r, at = R_MODB + 48 * L + 8 * v + k, 4 * (k % 4) + 2 * (k // 4)
                    ins = act.activation(mods[:, L, v, k, :], bank[7][:, at:at + 2], ACT.Identity, bias=par[:, r:r + 1])
                ins.then_inc(sem("mod_cols"), 1)

            def hcols(tag):
                L, n, v = norm_of(tag)
                act.wait_ge(sem("gsc"), 2 * L + n + 1)
                for k in range(0, KC, 2):
                    act.wait_ge(sem("turned"), 8 * nth(tag) + k + 1)
                    for s, lo, hi in stream_cols(tag):
                        ins = act.activation(hT[:, k, lo:hi], bank[0][:, lo:hi], ACT.Identity,
                                             bias=mods[:, L, v, k, s:s + 1], scale=gsc[:, L, n, k, s:s + 1])
                    ins.then_inc(sem("ht_0"), 1)

            def gate_rows(tag, streams):
                n = 0
                for s in streams:
                    for h in range(2):
                        act.wait_ge(sem("gate_mms"), gates_before(tag) + n + 1)
                        act.activation(GB[:, s, 512 * h:512 * h + 512], bank[4 + n % 2][:, :], ACT.Copy)\
                           .then_inc(sem("gate_rows"), 1)
                        n += 1

            def experts(L):
                if L == 0:
                    act.activation(YO[1], X[:, 0, 0:512], ACT.Copy).then_inc(sem("filler"), 1)
                    act.wait_ge(sem("filler"), 1)

                def body(g, tiles, skipped):
                    for q in range(2):
                        for s in tiles:
                            act.wait_ge(sem(f"gu_done_{s}"), 16 * L + 2 * g + q + 1)
                            act.activation(SG[s], bank[1 + s][:, 0:DE], ACT.Sigmoid).then_inc(sem(f"sg_{s}"), 1)
                        for s in tiles:
                            act.wait_ge(sem(f"he_turned_{s}"), 16 * L + 2 * g + q + 1)
                            act.activation(HET[s].rearrange("p f s -> p (f s)"), bank[3 + s][:, 0:DE], ACT.Copy)\
                               .then_inc(sem(f"het_{s}"), 1)
                    for s in tiles:
                        act.wait_ge(sem(f"down_done_{s}"), 16 * L + 2 * g + 2)
                        act.wait_ge(sem(f"y_free_{s}"), 8 * L + g + 1)
                        act.activation(YO[s], bank[5 + s][:, :], ACT.Copy).then_inc(sem(f"y_rows_{s}"), 1)
                    if skipped:
                        bump(act, skipped)

                group_loop(act, L, body, [("sg_1", 2), ("het_1", 2), ("y_rows_1", 1)])

            square_rows("a0")
            for i in range(2):
                mod_rows(i)
            hcols("a0")
            for m in range(4):
                act.wait_ge(sem("gate_mm"), m + 1)
                if m >= 2:
                    act.wait_ge(sem("glu_done"), m - 1)
                act.activation(SGL[m % 2], bank[2 * (m % 2) + 1][:, :], ACT.Sigmoid).then_inc(sem("glu_sig"), 1)
            act.wait_ge(sem("pads"), 2)
            for g in range(4):
                act.wait_ge(sem("pool_mm"), g + 1)
                act.activation(PP[:, g, :, PADP:PADP + HALF], bank[4 + g % 2][:, :].rearrange("p (s t) -> p s t", s=2), ACT.Copy)\
                   .then_inc(sem("pool_in"), 1)
            for i in range(2, 6):
                mod_rows(i)
            for g in range(4):
                act.wait_ge(sem("pool_mix"), g + 1)
                act.activation(mixT[:, 4 + g, :], bank[4 + g % 2][:, :], ACT.Identity, scale=par[:, R_PSC + g:R_PSC + g + 1])\
                   .then_inc(sem("pool_out"), 1)
            gate_rows("a0", (0, 1))
            for m in range(4):
                act.wait_ge(sem("ln_turned"), m + 1)
                if m >= 2:
                    act.wait_ge(sem("mix_done"), m - 1)
                gb = dict(bias=par[:, R_LNB + m:R_LNB + m + 1], scale=par[:, R_LNG + m:R_LNG + m + 1])
                act.activation(mixT[:, m, :], bank[m][:, :], ACT.Identity, **gb)
                act.activation(SGL[m % 2], bank[m][:, :], ACT.Sigmoid, **gb).then_inc(sem("ln_sig"), 1)
            for i in range(6, 12):
                mod_rows(i)
            square_rows("m0")
            hcols("m0")
            moe_scalar(act, 0, gate_rows, experts)
            square_rows("a1")
            hcols("a1")
            attention_scalar(act)
            gate_rows("a1", (1,))
            square_rows("m1")
            hcols("m1")
            moe_scalar(act, 1, gate_rows, experts)

        def attention_vector(dve, link):
            tt, ts, red = dve.tensor_tensor, dve.tensor_scalar, dve.tensor_reduce
            la = brow[:, B_LAM:B_LAM + 256].rearrange("p (a b d) -> p a b d", a=2, b=2)
            dve.wait_ge(sem("brow_in"), 64)
            dve.wait_ge(sem("ht_1"), 12)
            link(tt(lamp.rearrange("p (a d) -> p a d", a=2), la[:, :, 0, :], la[:, :, 1, :], ALU.mult))
            red(lam[:, 0:2], lamp.rearrange("p (a d) -> p a d", a=2), AX.X, ALU.add).then_inc(sem("lam_dots"), 1)
            ts(subs[:, 0:1], par[:, R_SUBG:R_SUBG + 1], 1.0 - LAM_INIT, None, ALU.mult).then_inc(sem("sub_scale"), 1)

            def rope(rows_, n, t, out_):
                r4 = rows_.rearrange("p (n a d) -> p n a d", n=n, a=2)
                cosb = C("cos", 32 * (t - 2), 32 * (t - 1)).unsqueeze(1).to_broadcast([P, 2 * n, 32])
                sinb = C("sin", 32 * (t - 2), 32 * (t - 1)).unsqueeze(1).to_broadcast([P, 2 * n, 32])
                flat = rows_.rearrange("p (n d) -> p n d", d=32)
                ac, as_ = RA[:, 0:64 * n], PT[1][:, 0:64 * n]
                tt(ac.rearrange("p (n d) -> p n d", d=32), flat, cosb, ALU.mult)
                link(tt(as_.rearrange("p (n d) -> p n d", d=32), flat, sinb, ALU.mult))
                c4 = ac.rearrange("p (n a d) -> p n a d", n=n, a=2)
                s4 = as_.rearrange("p (n a d) -> p n a d", n=n, a=2)
                o4 = out_.rearrange("p (n a d) -> p n a d", n=n, a=2)
                tt(o4[:, :, 0, :], c4[:, :, 0, :], s4[:, :, 1, :], ALU.subtract)
                return tt(o4[:, :, 1, :], c4[:, :, 1, :], s4[:, :, 0, :], ALU.add)

            for i, (kind, t, p) in enumerate(ITEMS):
                if kind == "vd":
                    continue
                c = count(i, NORMED)
                src = bank[i % 2]
                sq, qn, rt = SQ[c % 2], QN[c % 2], RT[c % 2]
                dve.wait_ge(sem("item_act"), i + 1)
                nseg = {"kd": 8, "qd": 8, "ckv": 1, "ql": 1, "qm": 2, "kvm": 2}[kind]
                wseg = {"kd": 64, "qd": 64, "ckv": 128, "ql": 256, "qm": 192, "kvm": 128}[kind]
                if kind == "ckv":
                    red(ssr[:, t:t + 1], sq[:, 128:192], AX.X, ALU.add)
                ins = red(ssq[:, 0:nseg], sq[:, 0:nseg * wseg].rearrange("p (n d) -> p n d", n=nseg), AX.X, ALU.add)
                if kind == "kvm":
                    link(ins)
                    ins = ts(ssq[:, 0:2], ssq[:, 0:2], ssr[:, t:t + 1], None, ALU.add)
                ins.then_inc(sem("ssq_ready"), 1)
                r = rs[:, 8 * (c % 2):8 * (c % 2) + nseg]
                if c >= 2:
                    dve.wait_ge(sem("cols_turned"), c - 1)
                if kind == "ckv":
                    ts_k = KR[:, t, :]
                    link(tt(ts_k, src[:, 128:192], brow[:, B_QKM + 192 + 128:B_QKM + 384], ALU.mult))
                    if t >= 2:
                        link(rope(ts_k, 1, t, ts_k))
                dve.wait_ge(sem("rs_ready"), c + 1)
                rb_ = r.unsqueeze(2).to_broadcast([P, nseg, wseg])
                if kind == "kvm":
                    two = src[:, :].rearrange("p (h d) -> p h d", h=2)[:, :, 0:P]
                    tt(qn[:, 0:256].rearrange("p (h d) -> p h d", h=2), two, rb_, ALU.mult).then_inc(sem("item_dve"), 1)
                    tt(rt.rearrange("p (h d) -> p h d", h=2), KR[:, t, :].unsqueeze(1).to_broadcast([P, 2, 64]),
                       r.unsqueeze(2).to_broadcast([P, 2, 64]), ALU.mult).then_inc(sem("rows_done"), 1)
                    continue
                ins = tt(qn[:, 0:nseg * wseg].rearrange("p (n d) -> p n d", n=nseg), src[:, 0:nseg * wseg].rearrange("p (n d) -> p n d", n=nseg), rb_, ALU.mult)
                ins.then_inc(sem("item_dve"), 1)
                dve.wait_ge(sem("item_dve"), c + 1)
                if kind in ("kd", "qd"):
                    g = brow[:, B_QKD + (64 if kind == "kd" else 0):B_QKD + (128 if kind == "kd" else 64)]
                    q3 = qn.rearrange("p (n d) -> p n d", n=8)
                    ins = tt(q3, q3, g.unsqueeze(1).to_broadcast([P, 8, 64]), ALU.mult)
                    if t >= 2:
                        link(ins)
                        ins = rope(qn, 8, t, qn)
                    ins.then_inc(sem("rows_done"), 1)
                elif kind == "qm":
                    link(tt(rt.rearrange("p (h d) -> p h d", h=2), qn[:, 0:384].rearrange("p (h d) -> p h d", h=2)[:, :, P:192],
                            brow[:, B_QKM + P:B_QKM + 192].unsqueeze(1).to_broadcast([P, 2, 64]), ALU.mult))
                    rope(rt, 2, t, rt).then_inc(sem("rows_done"), 1)
                else:
                    dve.nop()
                    dve.sem_inc(sem("rows_done"), 1)

            dve.wait_ge(sem("lam_exp"), 1)
            link(tt(lam[:, 4:5], lam[:, 3:4], lam[:, 2:3], ALU.subtract))
            link(ts(lam[:, 5:6], lam[:, 4:5], -LAM_INIT, None, ALU.add))
            n_units = len(UNITS)
            for i in range(n_units + 1):
                if i < n_units:
                    d = UNITS[i][0]
                    dve.wait_ge(sem("score_mm"), i + 1)
                    o = 2 * (i % 2)
                    for m in range(1 + d):
                        ins = red(mx[:, o + m:o + m + 1], bank[o + m][:, :], AX.X, ALU.max)
                    link(ins)
                    ts(nb[:, o:o + 1 + d], mx[:, o:o + 1 + d], -(MLA_SCALE, DIFF_SCALE)[d], None, ALU.mult).then_inc(sem("max_done"), 1)
                if i:
                    j = i - 1
                    d = UNITS[j][0]
                    o = 2 * (j % 2)
                    dve.wait_ge(sem("exp_done"), j + 1)
                    ins = dve.reciprocal(ri[:, o:o + 1 + d], es[:, o:o + 1 + d])
                    if d:
                        link(ins)
                        link(tt(ri[:, o + 1:o + 2], ri[:, o + 1:o + 2], lam[:, 5:6], ALU.mult))
                        link(ts(EX[:, j % 2, 0, :], EX[:, j % 2, 0, :], ri[:, o:o + 1], None, ALU.mult))
                        ins = dve.scalar_tensor_tensor(out=EX[:, j % 2, 0, :], in0=EX[:, j % 2, 1, :], scalar=ri[:, o + 1:o + 2],
                                                       in1=EX[:, j % 2, 0, :], op0=ALU.mult, op1=ALU.add)
                    ins.then_inc(sem("probs_ready"), 1)
                    dve.wait_ge(sem("probs_ready"), j + 1)
                    dve.wait_ge(sem("pv_mm"), j + 1)
                    if d:
                        dve.wait_ge(sem("o_rstd"), j - 7)
                        scale = ors[:, j % 2:j % 2 + 1]
                    else:
                        scale = ri[:, o:o + 1]
                    if j >= 2:
                        dve.wait_ge(sem("o_turned"), j - 1)
                    ts(OR[j % 2], bank[5][:, 0:P], scale, None, ALU.mult).then_inc(sem("o_rows"), 1)

        @block.vector
        def _(dve):
            link = Chain(dve, "vector_chain")
            tt, ts, red = dve.tensor_tensor, dve.tensor_scalar, dve.tensor_reduce

            dve.memset(cs[:, :, :], 0.0)
            dve.memset(YP[:, :, :, 0:PADC], 0.0)
            dve.memset(YP[:, :, :, PADC + HALF:], 0.0).then_inc(sem("pads"), 1)
            dve.memset(PP[:, :, :, 0:PADP], 0.0)
            dve.memset(PP[:, :, :, PADP + HALF:], 0.0).then_inc(sem("pads"), 1)
            dve.wait_ge(sem("pads"), 2)
            dve.wait_ge(sem("par_turned"), 1)
            dve.tensor_copy(par[:, 0:252], bank[7][:, 0:252])
            dve.tensor_copy(par[:, 256:294], bank[7][:, 256:294]).then_inc(sem("par_ready"), 1)
            dve.wait_ge(sem("par_ready"), 1)
            dve.wait_ge(sem("cs_sig"), 1)
            tt(cs[:, :, 0:2].rearrange("p k s -> p s k"), csg.rearrange("p (s k) -> p s k", s=2),
               par[:, R_CCTX:R_CCTX + 16].rearrange("p (s k) -> p s k", s=2), ALU.mult).then_inc(sem("cs_ready"), 1)

            def norm_scale(L, n):
                dve.wait_ge(sem("mod_cols"), 6 * L + (2 if n == 0 else 5))
                g = par[:, R_NORM + 16 * L + 8 * n:R_NORM + 16 * L + 8 * n + 8]
                for s in range(2):
                    ins = dve.scalar_tensor_tensor(out=gsc[:, L, n, :, s], in0=mods[:, L, 3 * n + 1, :, s], scalar=1.0, in1=g, op0=ALU.add, op1=ALU.mult)
                ins.then_inc(sem("gsc"), 1)

            def norm_rows(tag):
                L, n, v = norm_of(tag)
                dve.wait_ge(sem("rstd"), nth(tag) + 1)
                for t in x_tiles(tag):
                    ts(XS[:, t, :], X[:, t, :], rstd[:, t:t + 1], None, ALU.mult).then_inc(sem("xs"), 1)
                dve.wait_ge(sem("gsc"), 2 * L + n + 1)
                for k in range(1, KC, 2):
                    dve.wait_ge(sem("turned"), 8 * nth(tag) + k + 1)
                    for s, lo, hi in stream_cols(tag):
                        ins = ts(hT[:, k, lo:hi], bank[1][:, lo:hi], gsc[:, L, n, k, s:s + 1], mods[:, L, v, k, s:s + 1], ALU.mult, ALU.add)
                    ins.then_inc(sem("ht_1"), 1)

            def add_out(L, streams):
                nj = 2 * len(streams)
                dve.wait_ge(sem("gate_rows"), gates_before(f"a{L}") + 2 * len(streams))
                for h in range(2):
                    for j in range(nj):
                        i = h * nj + j
                        dve.wait_ge(sem("out_mm"), 8 * L + i + 1)
                        if i >= 2:
                            dve.wait_ge(sem("x_added"), 8 * L + i - 1)
                        tt(OUTT[i % 2], bank[i % 2][:, :], GB[:, streams[j // 2], 512 * h:512 * h + 512], ALU.mult).then_inc(sem("out_used"), 1)

            def route(L):
                nt, c, over, ntile = moe_plan(L)
                r = routing(L)
                dve.wait_ge(sem("scored"), L + 1)
                link(tt(r["biased"].rearrange("p (t e) -> p t e", t=nt), r["score"].rearrange("p (t e) -> p t e", t=nt),
                        brow[:, B_RB:B_RB + 32].unsqueeze(1).to_broadcast([P, nt, 32]), ALU.add))
                b4 = r["biased"].rearrange("p (g a b) -> p g a b", a=2, b=2)
                hi = r["hl"][:, 0:nt * 16].rearrange("p (g a) -> p g a", a=2)
                lo = r["hl"][:, nt * 16:nt * 32].rearrange("p (g a) -> p g a", a=2)
                m1, m2, m3 = (r["m12"][:, nt * 8 * i:nt * 8 * i + nt * 8] for i in range(3))
                tt(hi, b4[:, :, :, 0], b4[:, :, :, 1], ALU.max)
                link(tt(lo, b4[:, :, :, 0], b4[:, :, :, 1], ALU.min))
                tt(m1, hi[:, :, 0], hi[:, :, 1], ALU.max)
                tt(m2, hi[:, :, 0], hi[:, :, 1], ALU.min)
                link(tt(m3, lo[:, :, 0], lo[:, :, 1], ALU.max))
                link(tt(m2, m2, m3, ALU.max))
                link(tt(r["gs"], m1, m2, ALU.add))
                v8 = lambda x: x.rearrange("p (t g) -> p t g", t=nt)
                over8 = lambda x: x.unsqueeze(2).to_broadcast([P, nt, 8])
                link(red(r["gm"], v8(r["gs"]), AX.X, ALU.max))
                link(tt(v8(m1), v8(r["gs"]), over8(r["gm"]), ALU.is_equal))
                link(tt(v8(m2), v8(m1), C("gdown").unsqueeze(1).to_broadcast([P, nt, 8]), ALU.mult))
                link(red(r["gm"], v8(m2), AX.X, ALU.max))
                G = r["G"]
                tt(v8(G), v8(m2), over8(r["gm"]), ALU.is_equal).then_inc(sem("groups"), 1)
                dve.wait_ge(sem("groups"), L + 1)
                for src, dst in ((r["biased"], r["sel4"]), (r["score"], r["sc1"])):
                    link(tt(big[:, 0:nt * 32].rearrange("p (g e) -> p g e", e=4), src.rearrange("p (g e) -> p g e", e=4),
                            G.unsqueeze(2).to_broadcast([P, nt * 8, 4]), ALU.mult))
                    link(red(dst[:, 0:nt * 4].rearrange("p (t e) -> p t e", t=nt),
                             big[:, 0:nt * 32].rearrange("p (t g e) -> p t e g", t=nt, g=8), AX.X, ALU.add))
                s4 = r["sel4"][:, 0:nt * 4].rearrange("p (t e) -> p t e", t=nt)
                cmp_ = big[:, 0:nt * 16].rearrange("p (t e j) -> p t e j", t=nt, e=4)
                eq_ = big[:, 64:64 + nt * 16].rearrange("p (t e j) -> p t e j", t=nt, e=4)
                sj = s4.unsqueeze(2).to_broadcast([P, nt, 4, 4])
                se = s4.unsqueeze(3).to_broadcast([P, nt, 4, 4])
                tt(cmp_, sj, se, ALU.is_gt)
                link(tt(eq_, sj, se, ALU.is_equal))
                link(tt(eq_.rearrange("p t e j -> p t (e j)"), eq_.rearrange("p t e j -> p t (e j)"),
                        C("tie").unsqueeze(1).to_broadcast([P, nt, 16]), ALU.mult))
                link(tt(cmp_.rearrange("p t e j -> p (t e j)"), cmp_.rearrange("p t e j -> p (t e j)"), eq_.rearrange("p t e j -> p (t e j)"), ALU.add))
                w4 = r["w4"][:, 0:nt * 4]
                link(red(w4, cmp_.rearrange("p t e j -> p (t e) j"), AX.X, ALU.add))
                link(dve.scalar_tensor_tensor(out=w4, in0=w4, scalar=2.0, in1=r["sc1"][:, 0:nt * 4], op0=ALU.is_lt, op1=ALU.mult))
                w4t = w4.rearrange("p (t e) -> p t e", t=nt)
                link(red(r["wsum"], w4t, AX.X, ALU.add))
                link(dve.reciprocal(r["winv"], r["wsum"]))
                link(tt(w4t, w4t, r["winv"].unsqueeze(2).to_broadcast([P, nt, 4]), ALU.mult))
                dve.wait_ge(sem("ranks"), L + 1)
                nthr = nt * 2 - 1
                link(tt(big[:, 0:nt * 8], bank[5][:, 0:nt * 8], G, ALU.mult))
                link(red(r["rank"], v8(big[:, 0:nt * 8]), AX.X, ALU.add))
                no = nthr - (c - 1)
                link(tt(big[:, 0:8 * no].rearrange("p (g s) -> p g s", g=8), bank[5][:, 64:72].unsqueeze(2).to_broadcast([P, 8, no]),
                        C("thr", c - 1, nthr).unsqueeze(1).to_broadcast([P, 8, no]), ALU.is_gt))
                link(red(r["ov"], big[:, 0:8 * no].rearrange("p (g s) -> p g s", g=8), AX.X, ALU.add))
                link(tt(big[:, 0:64].rearrange("p (g j) -> p g j", g=8), C("before").rearrange("p (g j) -> p g j", g=8),
                        r["ov"].unsqueeze(1).to_broadcast([P, 8, 8]), ALU.mult))
                link(red(r["excl"], big[:, 0:64].rearrange("p (g j) -> p g j", g=8), AX.X, ALU.add))
                link(tt(big[:, 0:nt * nthr].rearrange("p (t s) -> p t s", t=nt), r["rank"].unsqueeze(2).to_broadcast([P, nt, nthr]),
                        C("thr", 0, nthr).unsqueeze(1).to_broadcast([P, nt, nthr]), ALU.is_ge))
                link(red(r["q"], big[:, 0:nt * nthr].rearrange("p (t s) -> p t s", t=nt), AX.X, ALU.add))
                link(dve.scalar_tensor_tensor(out=r["m"], in0=r["q"], scalar=-64.0, in1=r["rank"], op0=ALU.mult, op1=ALU.add))
                link(ts(r["isov"], r["q"], float(c), None, ALU.is_ge))
                for i, vec in enumerate((r["excl"], C("gup"))):
                    link(tt(v8(big[:, 0:nt * 8]), v8(G), vec.unsqueeze(1).to_broadcast([P, nt, 8]), ALU.mult))
                    link(red(r["tmp"][:, i * nt:(i + 1) * nt], v8(big[:, 0:nt * 8]), AX.X, ALU.add))
                ex, gid = r["tmp"][:, 0:nt], r["tmp"][:, nt:2 * nt]
                link(dve.scalar_tensor_tensor(out=ex, in0=gid, scalar=-float(c), in1=ex, op0=ALU.mult, op1=ALU.add))
                link(dve.scalar_tensor_tensor(out=ex, in0=ex, scalar=7.0 * c, in1=r["isov"], op0=ALU.add, op1=ALU.mult))
                link(dve.scalar_tensor_tensor(out=r["tile"], in0=gid, scalar=float(c), in1=r["q"], op0=ALU.mult, op1=ALU.add))
                link(tt(r["tile"], r["tile"], ex, ALU.add))
                link(dve.scalar_tensor_tensor(out=r["posf"], in0=r["tile"], scalar=float(ST), in1=r["m"], op0=ALU.mult, op1=ALU.add))
                dve.tensor_copy(smalli[:, 0:nt], r["posf"])
                if c == 2:
                    ts(smalli[:, 40:48], bank[5][:, 64:72], float(ST), None, ALU.is_gt)
                for t in range(nt):
                    ts(onehot[:, t * P:(t + 1) * P], C("iota64"), r["m"][:, t:t + 1], None, ALU.is_equal)
                    o = t * 5 * ntile
                    ts(brhs[:, o:o + ntile], C("iota", 0, ntile), r["tile"][:, t:t + 1], C("tok", t, t + 1), ALU.is_equal, ALU.mult)
                    for e in range(4):
                        ins = ts(brhs[:, o + (e + 1) * ntile:o + (e + 2) * ntile], C("iota", 0, ntile), r["tile"][:, t:t + 1],
                                 w4[:, 4 * t + e:4 * t + e + 1], ALU.is_equal, ALU.mult)
                ins.then_inc(sem("onehot"), 1)
                link(tt(r["excl"], r["excl"], r["ov"], ALU.add))
                link(tt(big[:, 0:8 * over].rearrange("p (j g) -> p j g", g=8), r["excl"].unsqueeze(1).to_broadcast([P, over, 8]),
                        C("iota", 0, over).unsqueeze(2).to_broadcast([P, over, 8]), ALU.is_le))
                link(red(r["gov"][:, 0:over], big[:, 0:8 * over].rearrange("p (j g) -> p j g", g=8), AX.X, ALU.add))
                ts(smalli[:, 26:26 + over], r["gov"][:, 0:over], float(GROUPS - 1), None, ALU.min)
                dve.tensor_copy(smalli[:, 33:34], r["excl"][:, 7:8])
                dve.wait_ge(sem("slots"), L + 1)
                for x in range(2):
                    dve.tensor_copy(cwt[ST * x:ST * x + ST, 0:2 * ntile].rearrange("p (n q) -> p q n", q=2),
                                    bank[6][ST * x:ST * x + ST, ntile:5 * ntile].rearrange("p (q x n) -> p x q n", q=2, x=2)[:, x])
                dve.tensor_copy(smalli[:, 4:4 + ntile], bank[6][:, 0:ntile]).then_inc(sem("slots_ready"), 1)

            def experts(L):
                c = moe_plan(L)[1]
                dve.wait_ge(sem("slots_ready"), L + 1)

                def body(g, tiles, skipped):
                    for s in tiles:
                        dve.wait_ge(sem(f"hg_turned_{s}"), 8 * L + g + 1)
                        dve.tensor_copy(HG[s].rearrange("p k s -> p (k s)"), bank[0][:, :]).then_inc(sem(f"hg_{s}"), 1)
                    for q in range(2):
                        for s in tiles:
                            dve.wait_ge(sem(f"sg_{s}"), 16 * L + 2 * g + q + 1)
                            dve.scalar_tensor_tensor(out=T1[s], in0=SG[s], scalar=cwt[:, bass.ds(2 * c * g + (2 * s + q), 1)],
                                                     in1=bank[1 + s][:, 0:DE], op0=ALU.mult, op1=ALU.mult).then_inc(sem(f"t1_{s}"), 1)
                            dve.wait_ge(sem(f"t1_{s}"), 16 * L + 2 * g + q + 1)
                            dve.tensor_tensor(HE[s], T1[s], bank[1 + s][:, DE:2 * DE], ALU.mult).then_inc(sem(f"he_{s}"), 1)
                    if skipped:
                        bump(dve, skipped)

                group_loop(dve, L, body, [("hg_1", 1), ("t1_1", 2), ("he_1", 2)])

            def add_moe(L):
                nt = moe_plan(L)[0]
                dve.wait_ge(sem("gate_rows"), gates_before(f"m{L}") + (4, 2)[L])
                for j in range(nt):
                    t = j if L == 0 else 2 + j
                    yg = B[:, j * D:(j + 1) * D]
                    dve.wait_ge(sem("y_gathered"), 64 * L + 16 * nt)
                    link(tt(yg, yg, GB[:, t // 2, :], ALU.mult))
                    tt(X[:, t, :], X[:, t, :], yg, ALU.add).then_inc(sem("x_done_a1" if L == 0 else "x_done_end"), 1)

            for s in range(2):
                dve.sem_inc(sem(f"he_{s}"), 1)
            norm_scale(0, 0)
            norm_rows("a0")
            for m in range(4):
                dve.wait_ge(sem("glu_sig"), m + 1)
                dve.wait_ge(sem("value_mm"), m + 1)
                s3 = lambda x: x.rearrange("p (s t) -> p s t", s=2)
                tt(YP[:, m, :, PADC:PADC + HALF], s3(bank[2 * (m % 2)][:, :]), s3(SGL[m % 2]), ALU.mult).then_inc(sem("glu_done"), 1)
                dve.wait_ge(sem("glu_done"), m + 1)
                for j in range(TAPS):
                    col = R_TAPS + 4 * j + m
                    src, w, acc = YP[:, m, :, j:j + HALF], par[:, col:col + 1], s3(ACC[j % 2])
                    if j >= 2:
                        dve.wait_ge(sem("tap_done"), m * TAPS + j - 1)
                    if j == 0:
                        ins = ts(acc, src, w, par[:, R_DWB + m:R_DWB + m + 1], ALU.mult, ALU.add)
                    elif j == 1:
                        ins = ts(acc, src, w, None, ALU.mult)
                    else:
                        ins = dve.scalar_tensor_tensor(out=acc, in0=src, scalar=w, in1=acc, op0=ALU.mult, op1=ALU.add)
                    ins.then_inc(sem("tap_done"), 1)
                dve.wait_ge(sem("tap_done"), (m + 1) * TAPS)
                tt(CV[:, m, :], ACC[0], ACC[1], ALU.add).then_inc(sem("conv_done"), 1)
                dve.wait_ge(sem("conv_done"), m + 1)
            for t in range(NT):
                dve.wait_ge(sem("conv_turned"), t + 1)
                link(dve.bn_stats(stats[:, 6 * t:6 * t + 6], bank[t][:, :]))
                dve.bn_aggr(mv[:, 2 * t:2 * t + 2], stats[:, 6 * t:6 * t + 6]).then_inc(sem("ln_stats"), 1)
            dve.wait_ge(sem("ln_rstd"), 1)
            for t in range(NT):
                ts(LNS[:, t, :], bank[t][:, :], mv[:, 2 * t:2 * t + 1], lrs[:, t:t + 1], ALU.subtract, ALU.mult).then_inc(sem("ln_rows"), 1)
            for m in range(4):
                dve.wait_ge(sem("ln_sig"), m + 1)
                tt(mixT[:, m, :], mixT[:, m, :], SGL[m % 2], ALU.mult).then_inc(sem("mix_done"), 1)
            add_out(0, (0, 1))
            norm_scale(0, 1)
            norm_rows("m0")
            route(0)
            experts(0)
            overflow_vector(dve, 0)
            add_moe(0)
            norm_scale(1, 0)
            norm_rows("a1")
            attention_vector(dve, link)
            add_out(1, (1,))
            norm_scale(1, 1)
            norm_rows("m1")
            route(1)
            experts(1)
            overflow_vector(dve, 1)
            add_moe(1)

        @block.gpsimd
        def _(pool):
            link = Chain(pool, "pool_chain")
            for s in range(2):
                pool.sem_inc(sem(f"y_free_{s}"), 1)

            pool.dma_start(cst[:, :], a["const"][:, 0:NCONST - 4 * HALF]).then_inc(sem("const_in"), 16)

            def power(dst, src, n, scale, name):
                link(pool.tensor_scalar(dst, src, scale, EPS, ALU.mult, ALU.add))
                pool.tensor_tensor(dst, dst, C("half", 0, 1).to_broadcast([P, n]), ALU.pow).then_inc(sem(name), 1)

            def rstd_of(tag):
                t = x_tiles(tag)
                pool.wait_ge(sem("ss"), 4 * nth(tag) + len(t))
                power(rstd[:, t[0]:], ss[:, t[0]:], len(t), 1.0 / D, "rstd")

            def add_out(L, tiles):
                for h in range(2):
                    for j, t in enumerate(tiles):
                        i = h * len(tiles) + j
                        pool.wait_ge(sem("out_used"), 8 * L + i + 1)
                        x = X[:, t, 512 * h:512 * h + 512]
                        pool.tensor_tensor(x, x, OUTT[i % 2], ALU.add).then_inc(sem("x_added"), 1)
                pool.wait_ge(sem("x_added"), 8 * L + 2 * len(tiles))
                pool.sem_inc(sem(f"x_done_m{L}"), 1)

            def experts(L):
                nt, c, over, ntile = moe_plan(L)
                for t in range(nt):
                    pool.wait_ge(sem("h2_rows"), 8 * L + 2 * t + 2)
                    pool.dma_start(h2d[t * P:(t + 1) * P, :], B[:, t * D:(t + 1) * D]).then_inc(sem("h2_stored"), 16)
                pool.wait_ge(sem("h2_stored"), 64 * L + 16 * nt)
                pool.wait_ge(sem("slots_ready"), L + 1)

                def store(g):
                    for s in range(c):
                        pool.wait_ge(sem(f"y_rows_{s}"), 8 * L + g + 2)
                        r = (g * c + s) * ST
                        for h in range(2):
                            pool.dma_start(yd[r:r + ST, 512 * h:512 * h + 512], YO[s][ST * h:ST * h + ST, :]).then_inc(sem(f"y_stored_{s}"), 16)
                    for s in range(c):
                        pool.wait_ge(sem(f"y_stored_{s}"), 256 * L + 32 * g + 32)
                        pool.sem_inc(sem(f"y_free_{s}"), 1)

                for g in range(GROUPS):
                    for s in range(c):
                        if g:
                            pool.wait_ge(sem(f"gathered_{s}"), 128 * L + 16 * g)
                            pool.wait_ge(sem(f"hg_turned_{s}"), 8 * L + g)
                        i = 4 + g * c + s
                        pool.indirect_dma_start(XG[s], None, h2d[:, :], bass.IndirectOffsetOnAxis(ap=smalli[0:ST, i:i + 1], axis=0))\
                            .then_inc(sem(f"gathered_{s}"), 16)
                    if g:
                        store(g - 1)
                store(GROUPS - 1)
                overflow_pool(pool, L)
                for j in range(nt):
                    pool.indirect_dma_start(B[:, j * D:(j + 1) * D], None, yd[:, :], bass.IndirectOffsetOnAxis(ap=smalli[:, j:j + 1], axis=0))\
                        .then_inc(sem("y_gathered"), 16)

            pool.wait_ge(sem("const_in"), 16)
            rstd_of("a0")
            pool.dma_start(rw[:, :, :], a["router_w"].rearrange("(k p) e -> p k e", p=P)).then_inc(sem("router_in"), 16)
            pool.dma_start(pw[:, :, :], a["pool_w"][0].rearrange("g c d -> c g d")).then_inc(sem("pool_w_in"), 16)
            for at, src in ((B_RB, a["router_b"]), (B_QKM, a["qk_g_mla"][0].rearrange("a d -> (a d)")),
                            (B_QKD, a["qk_g_diff"][0].rearrange("a d -> (a d)")), (B_LAM, a["diff_lambda"][0].rearrange("a d -> (a d)"))):
                n = src.shape[0]
                pool.dma_start(brow[:, at:at + n], src.partition_broadcast(P)).then_inc(sem("brow_in"), 16)
            pool.wait_ge(sem("turned"), KC)
            invcnt = B[:, 2048:2048 + 4 * HALF]
            pool.dma_start(invcnt, a["const"][:, NCONST - 4 * HALF:]).then_inc(sem("counts_in"), 16)
            pool.wait_ge(sem("counts_in"), 16)
            pool.wait_ge(sem("x_in"), 64)
            for t in range(3):
                r = GROUPS * 2 * ST + t * P
                pool.dma_start(yd[r:r + P, :], X[:, t, :]).then_inc(sem("y_filled"), 16)
            for g, w in enumerate(WINDOWS):
                pool.wait_ge(sem("pool_in"), g + 1)
                if g:
                    pool.wait_ge(sem("pooled"), g)
                src, k, width = PP[:, g, :, :], 1, 2 * PADP + HALF
                while k < w:
                    width -= k
                    dst = TA if src is not TA else TB
                    link(pool.tensor_tensor(dst[:, :, 0:width], src[:, :, 0:width], src[:, :, k:k + width], ALU.add))
                    src, k = dst, 2 * k
                dst = TA if src is not TA else TB
                s3 = mixT[:, g, :].rearrange("p (s t) -> p s t", s=2)
                link(pool.tensor_tensor(dst[:, :, 0:HALF], src[:, :, PADP - w // 2:PADP - w // 2 + HALF],
                                        invcnt[:, g * HALF:(g + 1) * HALF].unsqueeze(1).to_broadcast([P, 2, HALF]), ALU.mult))
                pool.tensor_tensor(s3, dst[:, :, 0:HALF], PP[:, g, :, PADP:PADP + HALF], ALU.subtract).then_inc(sem("pooled"), 1)
            pool.wait_ge(sem("ln_stats"), NT)
            link(pool.tensor_scalar(lrs[:, :], mv.rearrange("p (t a) -> p a t", a=2)[:, 1], EPS, None, ALU.add))
            pool.tensor_tensor(lrs[:, :], lrs[:, :], C("half", 0, 1).to_broadcast([P, 4]), ALU.pow).then_inc(sem("ln_rstd"), 1)
            pool.wait_ge(sem("y_filled"), 48)
            add_out(0, (0, 1, 2, 3))
            rstd_of("m0")
            experts(0)
            rstd_of("a1")
            for i, (kind, t, p) in enumerate(ITEMS):
                if kind == "vd":
                    continue
                c = count(i, NORMED)
                n = {"kd": 8, "qd": 8, "ckv": 1, "ql": 1, "qm": 2, "kvm": 2}[kind]
                w = {"kd": 64, "qd": 64, "ckv": 128, "ql": 256, "qm": 192, "kvm": 192}[kind]
                pool.wait_ge(sem("ssq_ready"), c + 1)
                r = rs[:, 8 * (c % 2):8 * (c % 2) + n]
                power(r, ssq[:, 0:n], n, 1.0 / w, "rs_ready")
            for i, (d, h, t) in enumerate(UNITS):
                if d:
                    pool.wait_ge(sem("o_squares"), i - 7)
                    power(ors[:, i % 2:i % 2 + 1], oss[:, i % 2:i % 2 + 1], 1, 1.0 / P, "o_rstd")
            add_out(1, (2, 3))
            rstd_of("m1")
            experts(1)
            o = out[0].rearrange("(i p) d -> i p d", p=P)
            for j in range(2):
                pool.wait_ge(sem("x_done_end"), j + 1)
                pool.dma_start(o[j], X[:, 2 + j, :]).then_inc(sem("out_stored"), 16)
            pool.wait_ge(sem("out_stored"), 32)


_INS = ["x", "c", "ctx", "c_ctx", "mod_w", "mod_b", "norm_g", "even_w_in", "conv_dw_w", "conv_dw_b", "conv_ln_g", "conv_ln_b",
        "pool_w", "pool_scale", "even_w_out", "odd_w_in", "mla_g_cq", "mla_w_uq", "mla_g_ckv", "mla_w_ukv", "qk_g_mla", "qk_g_diff",
        "diff_lambda", "diff_sub_g", "odd_w_out", "router_w", "router_b", "moe_w_gate", "moe_w_up", "moe_w_down"]


def kernel(**inputs):
    import concourse.bacc as bacc
    from concourse.bass_utils import run_bass_kernel_spmd

    nc = bacc.Bacc("TRN2", target_bir_lowering=False, num_devices=1)
    arrays, aps = {}, {}
    for name in _INS + ["const"]:
        v = constants() if name == "const" else np.ascontiguousarray(inputs[name])
        arrays[f"in_{name}"] = v
        aps[name] = nc.dram_tensor(f"in_{name}", v.shape, mybir.dt.from_np(v.dtype), kind="ExternalInput").ap()
    out = nc.dram_tensor("latents", (1, HALF, D), F32, kind="ExternalOutput").ap()
    generator_kernel(nc, aps, out)
    r = run_bass_kernel_spmd(nc, [arrays], core_ids=[0])
    return r.results[0]["latents"]
```

```python
from contextlib import ExitStack
import math

import numpy as np

import concourse.bass as bass
from concourse import mybir

P = 128
D = 1024
KC = D // P
NT = 4
HALF = 256
TOK = 512
N_MOD = 6
EPS = 1e-6
TAPS = 31
PADC = TAPS // 2
PADP = 8
WINDOWS = (2, 4, 8, 16)
GROUPS = 8
EPG = 4
EXPERTS = 32
DE = 256
ST = 64
RING = 6
LAM_INIT = 0.8 - 0.6 * math.exp(-0.3)
MLA_SCALE = (128 + 64) ** -0.5
DIFF_SCALE = 64 ** -0.5

ALU = mybir.AluOpType
ACT = mybir.ActivationFunctionType
AX = mybir.AxisListType
F32 = mybir.dt.float32
U32 = mybir.dt.uint32
I32 = mybir.dt.int32


def moe_plan(layer):
    tokens = TOK if layer == 0 else HALF
    c = 2 if layer == 0 else 1
    over = (tokens - c * ST) // ST
    return tokens // P, c, over, GROUPS * c + over


CONST = {}
_at = 0
for _name, _w in (("ident", 128), ("lower", 128), ("ones", 128), ("iota64", 128), ("sel", 4), ("sel32", 32), ("tok", 4), ("iota", 32),
                  ("gdown", 8), ("gup", 8), ("thr", 8), ("before", 64), ("tie", 16),
                  ("cos", 64), ("sin", 64), ("half", 4), ("invcnt", 4 * HALF)):
    CONST[_name] = (_at, _at + _w)
    _at += _w
NCONST = _at


def constants():
    a = np.zeros((P, NCONST), np.float32)

    def put(name, v):
        lo, hi = CONST[name]
        a[:, lo:hi] = v

    r = np.arange(P)
    put("ident", np.eye(P))
    put("lower", (r[:, None] < r[None, :]))
    put("ones", 1)
    put("iota64", np.arange(128) % 64)
    put("sel", (r[:, None] // 64 == np.arange(4)[None, :] // 2) & (r[:, None] % 32 == np.arange(4)[None, :] % 2))
    put("sel32", r[:, None] % 32 == np.arange(32)[None, :])
    put("tok", r[:, None] + 128 * np.arange(4)[None, :])
    put("iota", np.arange(32))
    put("gdown", 8 - np.arange(8))
    put("gup", np.arange(8))
    put("thr", 64 * (1 + np.arange(8)))
    put("before", (np.arange(8)[None, :] < np.arange(8)[:, None]).ravel())
    put("tie", (np.arange(4)[None, :] < np.arange(4)[:, None]).ravel())
    t = np.arange(HALF)
    cnt = [np.clip(t + w // 2, 0, HALF) - np.clip(t - w // 2, 0, HALF) for w in WINDOWS]
    put("invcnt", (1.0 / np.stack(cnt)).astype(np.float32).ravel())
    inv = (np.float32(10000.0) ** (-np.arange(0, 32, 2, dtype=np.float32) / np.float32(32))).astype(np.float32)
    row, col = (t // 64).astype(np.float32), (t % 64).astype(np.float32)
    ang = np.concatenate([row[:, None] * inv, col[:, None] * inv], -1)
    put("cos", np.cos(ang).astype(np.float32).reshape(2, P, 32).transpose(1, 0, 2).reshape(P, 64))
    put("sin", np.sin(ang).astype(np.float32).reshape(2, P, 32).transpose(1, 0, 2).reshape(P, 64))
    put("half", -0.5)
    return a


R_MODB, R_NORM = 0, 96
R_TAPS = 128
R_CCTX, R_C, R_DWB, R_LNG, R_LNB, R_PSC, R_GCQ, R_GCKV, R_SUBG, R_QN, R_KN = (
    256, 264, 272, 276, 280, 284, 288, 290, 291, 292, 293)
NROWS3 = 38
B_RB, B_QKM, B_QKD, B_LAM = 0, 32, 416, 544
NB = 800


def stream_plan():
    def pair(L, v):
        return [("mod", L, v, h) for h in (0, 1)]

    out = pair(0, 0) + pair(0, 1)
    out += [("win", j) for j in range(3)]
    for v in (2, 3, 4, 5):
        out += pair(0, v)
    out += [("wout", 0, 0)] + pair(1, 0) + [("wout", 0, 1)] + pair(1, 1) + pair(1, 2)
    moe0 = len(out)
    for q in range(GROUPS * 2):
        out += [("gu", 0, 2 * q), ("gu", 0, 2 * q + 1), ("down", 0, q)]
    out += pair(1, 3)
    for kind in OIN:
        out.append(("oin", kind))
    out.append(("lora",))
    out += pair(1, 4)
    out += [("wout", 1, h) for h in (0, 1)] + pair(1, 5)
    moe1 = len(out)
    for q in range(GROUPS * 2):
        out += [("gu", 1, 2 * q), ("gu", 1, 2 * q + 1), ("down", 1, q)]
    return out, (moe0, moe1)


OIN = {"ckv": (768, 960), "ql": (0, 256), "kd": (960, 1472), "qd": (256, 768), "vd": (1472, 1984)}


def generator_kernel(nc, a, out):
    STREAM, MOE_AT = stream_plan()
    where = {u: n for n, u in enumerate(STREAM)}
    with ExitStack() as ctx:
        def sb(name, shape, dt=F32):
            return ctx.enter_context(nc.sbuf_tensor(name, shape, dt))

        sems = {}

        def sem(name):
            if name not in sems:
                sems[name] = ctx.enter_context(nc.semaphore(name))
            return sems[name]

        cst = sb("cst", [P, NCONST - 4 * HALF])
        par = sb("par", [P, 294])
        brow = sb("brow", [P, NB])
        cs = sb("cs", [P, KC, 32])
        csg = sb("csg", [P, 16])
        mods = sb("mods", [P, 2, N_MOD, KC, 2])
        gsc = sb("gsc", [P, 2, 2, KC, 2])
        rw = sb("rw", [P, KC, EXPERTS])
        pw = sb("pw", [P, 4, P])
        X = sb("X", [P, NT, D])
        ring = sb("ring", [P, RING, 4096])
        hT = sb("hT", [P, KC, TOK])
        B = sb("B", [P, 4096])
        GB = sb("GB", [P, 2, D])
        MR = sb("MR", [P, 2, 512])
        rows = MR[:, 0, 0:384].rearrange("p (b d) -> p b d", b=3)
        WORK = sb("WORK", [P, 8704])
        small = sb("small", [P, 860])
        smalli = sb("smalli", [P, 48], U32)
        bank = [ctx.enter_context(nc.psum_tensor(f"bank{i}", [P, 512], F32)) for i in range(8)]
        h2d = nc.dram_tensor("h2_rows", (TOK, D), F32, kind="Internal").ap()
        yd = nc.dram_tensor("y_rows", (22 * ST, D), F32, kind="Internal").ap()

        def C(name, lo=0, hi=None):
            s, e = CONST[name]
            return cst[:, s + lo:(e if hi is None else s + hi)]

        ident = C("ident")
        used = [0]

        def cut(n):
            used[0] += n
            return small[:, used[0] - n:used[0]]

        ss = cut(4)
        rstd = cut(4)
        XS = B[:, :].rearrange("p (i d) -> p i d", i=NT)
        mixT = B[:, :].rearrange("p (m t) -> p m t", m=8)

        def slot(n, w=512):
            return ring[:, n % RING, 0:8 * w].rearrange("p (k n) -> p k n", k=8)

        def loaded(eng, n):
            eng.wait_ge(sem(f"weights_in{n % RING}"), 32 * (n // RING + 1))

        def passed(eng):
            eng.sem_inc(sem("passed"), 1)

        def load_sources(u):
            n = where[u]
            if u[0] == "mod":
                _, L, v, h = u
                c0 = v * D + h * 512
                src = a["mod_w"][L].rearrange("(k p) n -> p k n", p=P)
                s = slot(n)
                return [(s[:, :, 256 * i:256 * i + 256], src[:, :, c0 + 256 * i:c0 + 256 * i + 256]) for i in (0, 1)]
            if u[0] == "win":
                src = a["even_w_in"][0].rearrange("(k p) n -> p k n", p=P)
                s = slot(n)
                at = (256 * u[1], 512 + 256 * u[1]) if u[1] < 2 else (1024, 1280)
                return [(s[:, :, 256 * i:256 * i + 256], src[:, :, at[i]:at[i] + 256]) for i in (0, 1)]
            if u[0] == "wout":
                src = a["even_w_out" if u[1] == 0 else "odd_w_out"][0].rearrange("(k p) n -> p k n", p=P)
                s = slot(n)
                c0 = 512 * u[2]
                return [(s[:, :, 256 * i:256 * i + 256], src[:, :, c0 + 256 * i:c0 + 256 * i + 256]) for i in (0, 1)]
            if u[0] == "oin":
                lo, hi = OIN[u[1]]
                src = a["odd_w_in"][0].rearrange("(k p) n -> p k n", p=P)
                s = slot(n, hi - lo)
                return [(s[:, 4 * i:4 * i + 4, :], src[:, 4 * i:4 * i + 4, lo:hi]) for i in (0, 1)]
            if u[0] == "lora":
                flat = ring[:, n % RING, :]
                return [(flat[:, 0:1536].rearrange("p (k n) -> p k n", k=2),
                         a["mla_w_uq"][0].rearrange("(k p) n -> p k n", p=P)),
                        (flat[:, 1536:2560], a["mla_w_ukv"][0])]
            raise ValueError(u)

        def expert_sources(L, e, n, what):
            if what == "gu":
                s = slot(n)
                return [(s[:, :, 256 * i:256 * i + 256],
                         a[name][L, e].rearrange("(k p) n -> p k n", p=P)) for i, name in enumerate(("moe_w_gate", "moe_w_up"))]
            d = ring[:, n % RING, :].rearrange("p (x f n) -> p x f n", x=2, f=2)
            return [(d[:, i], a["moe_w_down"][L, e + i].rearrange("(f p) n -> p f n", p=P)) for i in (0, 1)]

        def routing(L):
            nt, c, over, ntile = moe_plan(L)
            base = used[0]

            r = {}
            for name, w in (("score", nt * 32), ("biased", nt * 32), ("hl", nt * 16 * 2), ("m12", nt * 8 * 3), ("gs", nt * 8),
                            ("gm", nt), ("G", nt * 8), ("sel4", nt * 8), ("w4", nt * 8), ("wsum", nt), ("winv", nt),
                            ("sc1", nt * 8), ("rank", nt), ("q", nt), ("m", nt), ("tile", nt), ("isov", nt), ("tmp", nt * 2), ("ov", 8),
                            ("excl", 8), ("posf", nt), ("gov", 8)):
                r[name] = cut(w)
            used[0] = base
            return r

        ITEMS = ([("ckv", t, 0) for t in range(4)] + [("ql", t, 0) for t in (2, 3)]
                 + [("kd", 0, 0), ("qd", 2, 0), ("kd", 1, 0), ("qd", 3, 0), ("kd", 2, 0), ("vd", 0, 0), ("kd", 3, 0)]
                 + [("vd", t, 0) for t in (1, 2, 3)]
                 + [("kvm", t, p) for t in range(4) for p in (0, 1)] + [("qm", t, p) for t in (2, 3) for p in (0, 1)])
        PBANK = (0, 1, 4, 5)
        UNITS = [(d, h, t) for d in (0, 1) for h in range(4) for t in range(2)]

        wk = WORK
        big = wk[:, 0:1024]
        onehot = wk[:, 1024:1536]
        brhs = wk[:, 1536:1536 + 4 * 110]
        cwt = wk[:, 2048:2048 + 44]
        XG = [wk[0:ST, 2112 + 1024 * i:3136 + 1024 * i] for i in (0, 1)]
        HG = [wk[:, 4160 + 512 * i:4672 + 512 * i].rearrange("p (k s) -> p k s", k=KC) for i in (0, 1)]
        SG = [wk[:, 5184 + 256 * i:5440 + 256 * i] for i in (0, 1)]
        T1 = [wk[:, 5696 + 256 * i:5952 + 256 * i] for i in (0, 1)]
        HE = [wk[:, 6208 + 256 * i:6464 + 256 * i] for i in (0, 1)]
        HET = [wk[:, 6720 + 256 * i:6976 + 256 * i].rearrange("p (f s) -> p f s", f=2) for i in (0, 1)]
        YO = [wk[:, 7232 + 512 * i:7744 + 512 * i] for i in (0, 1)]

        YP = wk[:, 0:2288].rearrange("p (m s t) -> p m s t", m=4, s=2)
        PP = wk[:, 2288:2288 + 2176].rearrange("p (g s t) -> p g s t", g=4, s=2)
        CV = wk[:, 4464:4464 + 2048].rearrange("p (m t) -> p m t", m=4)
        ACC = [wk[:, 6512 + 512 * i:7024 + 512 * i] for i in (0, 1)]
        SGL = [wk[:, 7536 + 512 * i:8048 + 512 * i] for i in (0, 1)]
        TA = GB[:, 0, 0:544].rearrange("p (s t) -> p s t", s=2)
        TB = GB[:, 1, 0:544].rearrange("p (s t) -> p s t", s=2)
        LNS = hT[:, 0:4, :]
        stats = cut(24)
        mv = cut(8)
        lrs = cut(4)

        class Chain:

            def __init__(self, eng, name):
                self.eng, self.s, self.n = eng, sem(name), 0

            def __call__(self, ins):
                self.n += 1
                ins.then_inc(self.s, 1)
                self.eng.wait_ge(self.s, self.n)

        block = ctx.enter_context(nc.Block())

        MOD_PAIRS = [u[1:3] for u in STREAM if u[0] == "mod" and u[3] == 0]

        def freed(n):
            u = STREAM[n]
            if u[0] == "mod":
                return "mod_mm", MOD_PAIRS.index(u[1:3]) + 1
            if u[0] == "win":
                return ("value_mm", 2 * u[1] + 2) if u[1] < 2 else ("pool_mm", 4)
            if u[0] == "wout":
                return "out_mm", 8 * u[1] + (u[2] + 1) * (4, 2)[u[1]]
            if u[0] == "oin":
                return "proj_mm", 1 + max(i for i, it in enumerate(ITEMS) if it[0] == u[1])
            if u[0] == "lora":
                return "proj_mm", len(ITEMS)
            if u[0] == "gu":
                return "gu_done", 16 * u[1] + u[2] // 2 + 1
            return "down_done", 16 * u[1] + u[2] + 1

        QN = [wk[:, 512 * i:512 * i + 512] for i in (0, 1)]
        SQ = [wk[:, 1024 + 512 * i:1536 + 512 * i] for i in (0, 1)]
        KR = wk[:, 2048:2304].rearrange("p (t d) -> p t d", t=4)
        kTr = wk[:, 2304:3328].rearrange("p (a t) -> p a t", a=2)
        qTn = wk[:, 3328:4352].rearrange("p (h t) -> p h t", h=4)
        qTr = wk[:, 4352:4864].rearrange("p (a t) -> p a t", a=2)
        qdT = wk[:, 4864:5888].rearrange("p (h t) -> p h t", h=4)
        cqT = wk[:, 5888:6400].rearrange("p (k t) -> p k t", k=2)
        ckvT = wk[:, 6400:6912]
        PT = [wk[:, 6912 + 512 * i:7424 + 512 * i] for i in (0, 1)]
        RA = wk[:, 6912:7424]
        OR = [wk[:, 7936 + 128 * i:8064 + 128 * i] for i in (0, 1)]
        RT = [wk[:, 8192 + 128 * i:8320 + 128 * i] for i in (0, 1)]
        kTn = hT[:, 0:4, :]
        VM = hT[:, 4:8, :]
        kdT = B[:, 0:2048].rearrange("p (h t) -> p h t", h=4)
        oT = B[:, 2048:4096].rearrange("p (c t) -> p c t", c=8)
        VD = X[:, 0:2, :].rearrange("p a (b d) -> p (a b) d", b=2)
        EX = GB[:, :, :].rearrange("p a (b d) -> p a b d", b=2)
        ssq = cut(16)
        rs = cut(16)
        ssr = cut(4)
        mx = cut(4)
        nb = cut(4)
        es = cut(4)
        ri = cut(8)
        oss = cut(2)
        ors = cut(2)
        lam = cut(8)
        subs = cut(1)
        lamp = OR[0]
        OUTT = [wk[:, 6512 + 512 * i:7024 + 512 * i] for i in (0, 1)]

        def count(i, kinds):
            return sum(it[0] in kinds for it in ITEMS[:i])

        OUT_BANKS = ((4, 5), (0, 1))
        NORMED = ("kd", "ckv", "ql", "qd", "qm", "kvm")
        BLOCKS = {"kd": 4, "qd": 4, "ckv": 1, "ql": 2, "qm": 3, "kvm": 3}

        def project_pe(pe, loaded, mod_multiply):

            def source(i):
                kind, t, p = ITEMS[i]
                if i >= 4:
                    pe.wait_ge(sem("item_act"), i - 3)
                    if count(i - 3, NORMED):
                        pe.wait_ge(sem("item_dve"), count(i - 3, NORMED))
                dst = bank[PBANK[i % 4]]
                if kind in OIN:
                    lo, hi = OIN[kind]
                    n = where[("oin", kind)]
                    if t == (2 if kind in ("ql", "qd") else 0):
                        loaded(pe, n)
                    w = slot(n, hi - lo)
                    for k in range(KC):
                        mm = pe.matmul(dst[:, 0:hi - lo], hT[:, k, t * P:(t + 1) * P], w[:, k, :], start=k == 0, stop=k == KC - 1)
                else:
                    n = where[("lora",)]
                    flat = ring[:, n % RING, :]
                    if kind == "kvm" and t == 0 and p == 0:
                        loaded(pe, n)
                        pe.wait_ge(sem("cols"), sum(it[0] in ("ckv", "ql") for it in ITEMS))
                    if kind == "qm":
                        for k in range(2):
                            mm = pe.matmul(dst[:, 0:384], cqT[:, k, (t - 2) * P:(t - 1) * P],
                                           flat[:, 768 * k + 384 * p:768 * k + 384 * p + 384], start=k == 0, stop=k == 1)
                    else:
                        mm = pe.matmul(dst[:, :], ckvT[:, t * P:(t + 1) * P], flat[:, 1536 + 512 * p:2048 + 512 * p],
                                       start=True, stop=True)
                mm.then_inc(sem("proj_mm"), 1)

            def turn(i):
                kind, t, p = ITEMS[i]
                if kind == "vd":
                    return
                c = count(i, NORMED)
                if c >= 2:
                    pe.wait_ge(sem("cols"), c - 1)
                pe.wait_ge(sem("rows_done"), c + 1)
                for b in range(BLOCKS[kind]):
                    src = QN[c % 2][:, b * P:(b + 1) * P]
                    if kind == "qm":
                        src = QN[c % 2][:, 192 * b:192 * b + P] if b < 2 else RT[c % 2]
                    if kind == "kvm" and b == 2:
                        src = RT[c % 2]
                    mm = pe.transpose(bank[2 + c % 2][:, b * P:(b + 1) * P], src, ident)
                mm.then_inc(sem("cols_turned"), 1)

            for i in range(len(ITEMS) + 2):
                if i < len(ITEMS):
                    source(i)
                elif i == len(ITEMS):
                    mod_multiply(10)
                if i >= 2:
                    turn(i - 2)

        def attention_pe(pe):
            pe.wait_ge(sem("cols"), count(99, NORMED))
            n_units = len(UNITS)

            def scores(i):
                d, h, t = UNITS[i]
                if i >= 2:
                    pe.wait_ge(sem("exp_done"), i - 1)
                b0 = bank[2 * (i % 2)]
                q = slice(t * P, (t + 1) * P)
                if not d:
                    r = 64 * (h % 2)
                    pe.matmul(b0[:, :], qTn[:, h, q], kTn[:, h, :], start=True, stop=False)
                    mm = pe.matmul(b0[:, :], qTr[r:r + 64, h // 2, q], kTr[r:r + 64, h // 2, :], start=False, stop=True)
                else:
                    for m in range(2):
                        mm = pe.matmul(bank[2 * (i % 2) + m][:, :], qdT[64 * m:64 * m + 64, h, q], kdT[64 * m:64 * m + 64, h, :],
                                       start=True, stop=True)
                mm.then_inc(sem("score_mm"), 1)

            def probs(i):
                pe.wait_ge(sem("probs_ready"), i + 1)
                if i:
                    pe.wait_ge(sem("pt_done"), i)
                for c in range(4):
                    mm = pe.transpose(bank[4][:, c * P:(c + 1) * P], EX[:, i % 2, 0, c * P:(c + 1) * P], ident)
                mm.then_inc(sem("probs_turned"), 1)

            def values(i):
                d, h, t = UNITS[i]
                pe.wait_ge(sem("pt_done"), i + 1)
                if i:
                    pe.wait_ge(sem("o_rows"), i)
                v = VD if d else VM
                for c in range(4):
                    mm = pe.matmul(bank[5][:, 0:P], PT[i % 2][:, c * P:(c + 1) * P], v[:, c, h * P:(h + 1) * P], start=c == 0, stop=c == 3)
                mm.then_inc(sem("pv_mm"), 1)

            def turn_o(i):
                pe.wait_ge(sem("o_rows"), i + 1)
                if i:
                    pe.wait_ge(sem("o_cols"), i)
                else:
                    pe.wait_ge(sem("mod_rows"), 11)
                pe.transpose(bank[6][:, 0:P], OR[i % 2], ident).then_inc(sem("o_turned"), 1)

            for i in range(n_units + 3):
                if i < n_units:
                    scores(i)
                if 0 <= i - 2 < n_units:
                    values(i - 2)
                if 0 <= i - 3:
                    turn_o(i - 3)
                if 0 <= i - 1 < n_units:
                    probs(i - 1)

        def attention_scalar(act, mod_copy):
            def cols(i):
                kind, t, p = ITEMS[i]
                if kind == "vd":
                    return
                c = count(i, NORMED)
                act.wait_ge(sem("cols_turned"), c + 1)
                src = bank[2 + c % 2]
                tk, tq = slice(t * P, (t + 1) * P), slice((t - 2) * P, (t - 1) * P)
                four = src[:, :].rearrange("p (h t) -> p h t", h=4)
                if kind == "kd":
                    ins = act.activation(kdT[:, :, tk], four, ACT.Copy)
                elif kind == "qd":
                    ins = act.activation(qdT[:, :, tq], four, ACT.Copy)
                elif kind == "ckv":
                    ins = act.activation(ckvT[:, tk], src[:, 0:P], ACT.Identity, scale=par[:, R_GCKV:R_GCKV + 1])
                elif kind == "ql":
                    for k in range(2):
                        ins = act.activation(cqT[:, k, tq], src[:, k * P:(k + 1) * P], ACT.Identity, scale=par[:, R_GCQ + k:R_GCQ + k + 1])
                elif kind == "qm":
                    act.activation(qTn[:, 2 * p:2 * p + 2, tq], four[:, 0:2, :], ACT.Identity, scale=par[:, R_QN:R_QN + 1])
                    ins = act.activation(qTr[:, p, tq], four[:, 2, :], ACT.Copy)
                else:
                    act.activation(kTn[:, 2 * p:2 * p + 2, tk], four[:, 0:2, :], ACT.Identity, scale=par[:, R_KN:R_KN + 1])
                    ins = act.activation(kTr[:, p, tk], four[:, 2, :], ACT.Copy)
                ins.then_inc(sem("cols"), 1)

            for i, (kind, t, p) in enumerate(ITEMS):
                if i == 2:
                    act.wait_ge(sem("lam_dots"), 1)
                    act.wait_ge(sem("sub_scale"), 1)
                    act.activation(lam[:, 2:4], lam[:, 0:2], ACT.Exp).then_inc(sem("lam_exp"), 1)
                act.wait_ge(sem("proj_mm"), i + 1)
                src = bank[PBANK[i % 4]]
                c = count(i, NORMED)
                if kind != "vd" and c >= 2:
                    act.wait_ge(sem("ssq_ready"), c - 1)
                if kind == "vd":
                    act.wait_ge(sem("xs"), 12)
                    ins = act.activation(VD[:, t, :], src[:, :], ACT.Copy)
                elif kind == "kvm":
                    two = src[:, :].rearrange("p (h d) -> p h d", h=2)
                    act.activation(VM[:, t, 256 * p:256 * p + 256].rearrange("p (h d) -> p h d", h=2), two[:, :, P:2 * P], ACT.Copy)
                    ins = act.activation(SQ[c % 2][:, 0:256].rearrange("p (h d) -> p h d", h=2), two[:, :, 0:P], ACT.Square)
                else:
                    w = {"kd": 512, "qd": 512, "ckv": 192, "ql": 256, "qm": 384}[kind]
                    ins = act.activation(SQ[c % 2][:, 0:w], src[:, 0:w], ACT.Square)
                ins.then_inc(sem("item_act"), 1)
                if i >= 2:
                    cols(i - 2)
            for i in (2, 1):
                cols(len(ITEMS) - i)
            mod_copy(10)
            n_units = len(UNITS)

            def exps(i):
                d = UNITS[i][0]
                act.wait_ge(sem("max_done"), i + 1)
                if i >= 2:
                    act.wait_ge(sem("probs_turned"), i - 1)
                for m in range(1 + d):
                    ins = act.activation(EX[:, i % 2, m, :], bank[2 * (i % 2) + m][:, :], ACT.Exp, bias=nb[:, 2 * (i % 2) + m:2 * (i % 2) + m + 1],
                                         scale=(MLA_SCALE, DIFF_SCALE)[d], accum_out=es[:, 2 * (i % 2) + m:2 * (i % 2) + m + 1])
                ins.then_inc(sem("exp_done"), 1)

            def o_cols(i):
                d, h, t = UNITS[i]
                act.wait_ge(sem("o_turned"), i + 1)
                scale = subs[:, 0:1] if d else 1.0
                act.activation(oT[:, 4 * d + h, t * P:(t + 1) * P], bank[6][:, 0:P], ACT.Identity, scale=scale).then_inc(sem("o_cols"), 1)

            def o_squares(i):
                j = i % 2
                act.wait_ge(sem("pv_mm"), i + 1)
                if i >= 2:
                    act.wait_ge(sem("o_turned"), i - 1)
                act.activation(OR[j], bank[5][:, 0:P], ACT.Square, accum_out=oss[:, j:j + 1]).then_inc(sem("o_squares"), 1)

            def turned_probs(i):
                act.wait_ge(sem("probs_turned"), i + 1)
                if i >= 2:
                    act.wait_ge(sem("pv_mm"), i - 1)
                act.activation(PT[i % 2], bank[4][:, :], ACT.Copy).then_inc(sem("pt_done"), 1)

            for i in range(n_units + 3):
                if 0 <= i - 2 < n_units and UNITS[i - 2][0]:
                    o_squares(i - 2)
                if i < n_units:
                    exps(i)
                if 0 <= i - 3:
                    o_cols(i - 3)
                if 0 <= i - 1 < n_units:
                    turned_probs(i - 1)

        def moe_scalar(act, L, gate_rows, experts):
            nt, c, over, ntile = moe_plan(L)
            act.wait_ge(sem("logit_parts"), L + 1)
            act.activation(MR[:, 0, 0:nt * P], bank[6][:, 0:nt * P], ACT.Copy).then_inc(sem("logit_rows"), 1)
            act.wait_ge(sem("logits"), L + 1)
            act.activation(routing(L)["score"], bank[2][:, 0:nt * 32], ACT.Sigmoid).then_inc(sem("scored"), 1)
            for i in range(2 * nt):
                act.wait_ge(sem("h2_turned"), 8 * L + i + 1)
                act.activation(B[:, 512 * i:512 * i + 512], bank[3 + i % 2][:, :], ACT.Copy).then_inc(sem("h2_rows"), 1)
            if L == 1:
                gate_rows("m1", (1,), (3, 4))
            experts(L)
            overflow_scalar(act, L)

        def group_loop(eng, L, body, skipped):
            c = moe_plan(L)[1]
            eng.wait_ge(sem("slots_ready"), L + 1)
            with eng.Fori(0, GROUPS) as g:
                if c == 1:
                    body(g, (0,), None)
                else:
                    two = eng.value_load(smalli[0:1, bass.ds(g + 40, 1)], min_val=0, max_val=1)
                    with eng.If(two > 0):
                        body(g, (0, 1), None)
                    with eng.Else():
                        body(g, (0,), skipped)

        def expert_slot_freed(eng, L, done, v):
            for s in range(moe_plan(L)[1]):
                eng.wait_ge(sem(f"{done}_{s}"), v)

        def bump(eng, names):
            for name, n in names:
                eng.sem_inc(sem(name), n)

        def overflow_count(eng, L):
            eng.wait_ge(sem("slots_ready"), L + 1)
            return eng.value_load(smalli[0:1, 33:34], min_val=0, max_val=moe_plan(L)[2])

        gu_over = hT[:, :, :]
        dn_over = B[:, :].rearrange("p (x f n) -> p x f n", x=2, f=2)

        def overflow_scalar(act, L):
            n = overflow_count(act, L)
            with act.If(n > 0):
                act.sem_inc(sem(f"over_rows{L}"), 1)
                with act.Fori(0, n) as j:
                    for q in range(2):
                        act.wait_ge(sem(f"over_gu{L}"), 4 * j + 2 * q + 3)
                        act.activation(SG[0], bank[1][:, 0:DE], ACT.Sigmoid).then_inc(sem(f"over_sg{L}"), 1)
                        act.wait_ge(sem(f"over_he_turned{L}"), 2 * j + q + 1)
                        act.activation(HET[0].rearrange("p f s -> p (f s)"), bank[3][:, 0:DE], ACT.Copy).then_inc(sem(f"over_het{L}"), 1)
                    act.wait_ge(sem(f"over_down{L}"), 2 * j + 3)
                    act.activation(YO[0], bank[5][:, :], ACT.Copy).then_inc(sem(f"over_rows{L}"), 1)
            with act.Else():
                act.nop()
            act.nop()

        def overflow_pe(pe, L):
            n = overflow_count(pe, L)
            with pe.If(n > 0):
                for name in ("over_gu", "over_down"):
                    pe.sem_inc(sem(f"{name}{L}"), 1)
                with pe.Fori(0, n) as j:
                    pe.wait_ge(sem(f"over_gathered{L}"), 16 * j + 16)
                    passed(pe)
                    for k in range(KC):
                        mm = pe.transpose(bank[0][:, k * ST:(k + 1) * ST], XG[0][:, k * P:(k + 1) * P], ident[0:ST, 0:ST])
                    mm.then_inc(sem(f"over_turned{L}"), 1)
                    pe.wait_ge(sem(f"over_hg{L}"), j + 1)
                    for q in range(2):
                        pe.wait_ge(sem(f"over_he{L}"), 2 * j + q + 1)
                        for x in range(2):
                            pe.wait_ge(sem(f"over_gu_in{L}"), 128 * j + 64 * q + 32 * x + 32)
                            for k in range(KC):
                                mm = pe.matmul(bank[1][ST * x:ST * x + ST, :], HG[0][:, k, :], gu_over[:, k, :], start=k == 0, stop=k == KC - 1)
                            mm.then_inc(sem(f"over_gu{L}"), 1)
                        pe.wait_ge(sem(f"over_he{L}"), 2 * j + q + 2)
                        for f in range(2):
                            mm = pe.transpose(bank[3][:, f * P:(f + 1) * P], HE[0][:, f * P:(f + 1) * P], ident)
                        mm.then_inc(sem(f"over_he_turned{L}"), 1)
                        pe.wait_ge(sem(f"over_het{L}"), 2 * j + q + 1)
                        pe.wait_ge(sem(f"over_down_in{L}"), 64 * j + 32 * q + 32)
                        if q == 0:
                            pe.wait_ge(sem(f"over_rows{L}"), j + 1)
                        for f in range(2):
                            for x in range(2):
                                for h in range(2):
                                    mm = pe.matmul(bank[5][ST * h:ST * h + ST, :], HET[0][:, f, ST * x:ST * x + ST],
                                                   dn_over[:, x, f, 512 * h:512 * h + 512],
                                                   start=q == 0 and f == 0 and x == 0, stop=q == 1 and f == 1 and x == 1)
                        mm.then_inc(sem(f"over_down{L}"), 1)
            with pe.Else():
                pe.nop()
            pe.nop()

        def overflow_vector(dve, L):
            c = moe_plan(L)[1]
            n = overflow_count(dve, L)
            with dve.If(n > 0):
                dve.sem_inc(sem(f"over_he{L}"), 1)
                with dve.Fori(0, n) as j:
                    dve.wait_ge(sem(f"over_turned{L}"), j + 1)
                    dve.tensor_copy(HG[0].rearrange("p k s -> p (k s)"), bank[0][:, :]).then_inc(sem(f"over_hg{L}"), 1)
                    for q in range(2):
                        dve.wait_ge(sem(f"over_sg{L}"), 2 * j + q + 1)
                        dve.scalar_tensor_tensor(out=T1[0], in0=SG[0], scalar=cwt[:, bass.ds(2 * j + (16 * c + q), 1)],
                                                 in1=bank[1][:, 0:DE], op0=ALU.mult, op1=ALU.mult).then_inc(sem(f"over_t1{L}"), 1)
                        dve.wait_ge(sem(f"over_t1{L}"), 2 * j + q + 1)
                        dve.tensor_tensor(HE[0], T1[0], bank[1][:, DE:2 * DE], ALU.mult).then_inc(sem(f"over_he{L}"), 1)
            with dve.Else():
                dve.nop()
            dve.nop()

        def overflow_pool(pool, L):
            c = moe_plan(L)[1]
            n = overflow_count(pool, L)
            with pool.If(n > 0):
                with pool.Fori(0, n) as j:
                    pool.tensor_copy(smalli[0:ST, 34:35], smalli[0:ST, bass.ds(j + (4 + 8 * c), 1)]).then_inc(sem(f"over_index{L}"), 1)
                    pool.wait_ge(sem(f"over_index{L}"), j + 1)
                    passed(pool)
                    pool.indirect_dma_start(XG[0], None, h2d[:, :], bass.IndirectOffsetOnAxis(ap=smalli[0:ST, 34:35], axis=0))\
                        .then_inc(sem(f"over_gathered{L}"), 16)
                    grp = pool.value_load(smalli[0:1, bass.ds(j + 26, 1)], min_val=0, max_val=GROUPS - 1)
                    for q in range(2):
                        for x in range(2):
                            pool.wait_ge(sem(f"over_gu{L}"), 4 * j + 2 * q + x + 1)
                            passed(pool)
                            for i, name in enumerate(("moe_w_gate", "moe_w_up")):
                                pool.dma_start(gu_over[:, :, 256 * i:256 * i + 256],
                                               a[name][L, grp * EPG + 2 * q + x].rearrange("(k p) n -> p k n", p=P)).then_inc(sem(f"over_gu_in{L}"), 16)
                        pool.wait_ge(sem(f"over_down{L}"), 2 * j + q + 1)
                        passed(pool)
                        for x in range(2):
                            pool.dma_start(dn_over[:, x], a["moe_w_down"][L, grp * EPG + 2 * q + x].rearrange("(f p) n -> p f n", p=P))\
                                .then_inc(sem(f"over_down_in{L}"), 16)
                    pool.wait_ge(sem(f"over_rows{L}"), j + 2)
                    passed(pool)
                    for h in range(2):
                        pool.dma_start(yd[bass.ds(j * ST + 8 * c * ST, ST), 512 * h:512 * h + 512], YO[0][ST * h:ST * h + ST, :])\
                            .then_inc(sem(f"over_stored{L}"), 16)
                    pool.wait_ge(sem(f"over_stored{L}"), 32 * j + 32)
            with pool.Else():
                pool.nop()
            pool.nop()

        def nth(tag):
            return ("a0", "m0", "a1", "m1").index(tag)

        def gates_before(tag):
            return {"a0": 0, "m0": 4, "a1": 8, "m1": 10}[tag]

        def x_tiles(tag):
            return (2, 3) if tag == "m1" else (0, 1, 2, 3)

        def norm_of(tag):
            return int(tag[1]), int(tag[0] == "m"), 3 * int(tag[0] == "m")

        def stream_cols(tag):
            return [(1, 0, 256)] if tag == "m1" else [(0, 0, 256), (1, 256, 512)]

        @block.sync
        def _(sp):
            def load(n, pairs):
                if n >= RING:
                    s, v = freed(n - RING)
                    if s in ("gu_done", "down_done"):
                        expert_slot_freed(sp, STREAM[n - RING][1], s, v)
                    else:
                        sp.wait_ge(sem(s), v)
                for dst, src in pairs:
                    sp.dma_start(dst, src).then_inc(sem(f"weights_in{n % RING}"), 16)

            sp.dma_start(rows[96:128, 0, :], a["norm_g"].rearrange("i n (c p) -> (i n c) p", p=P)).then_inc(sem("rows_in"), 16)
            sp.dma_start(rows[0:96, 0, :], a["mod_b"].rearrange("i (v p) -> (i v) p", p=P)).then_inc(sem("rows_in"), 16)
            sp.dma_start(rows[0:124, 1, :], a["conv_dw_w"][0].rearrange("t (c p) -> (t c) p", p=P)).then_inc(sem("rows_in"), 16)

            for n, u in enumerate(STREAM):
                if n == 1:
                    sp.wait_ge(sem("rows_in"), 16 * 14)
                if n in (3, 4):
                    tokens = a[("ctx", "x")[n - 3]][0].rearrange("(i p) d -> i p d", p=P)
                    for i in range(2):
                        sp.dma_start(X[:, 2 * (n - 3) + i, :], tokens[i]).then_inc(sem("x_in"), 16)
                if u[0] in ("gu", "down") and n == MOE_AT[u[1]] + 4:
                    sp.wait_ge(sem("gathered_0"), 128 * u[1] + 16)
                if u == ("oin", "kd"):
                    for i in range(2):
                        sp.wait_ge(sem(f"y_gathered_{i}"), 32)
                if u[0] not in ("gu", "down"):
                    load(n, load_sources(u))
                elif n < MOE_AT[u[1]] + RING:
                    load(n, expert_sources(u[1], u[2] * (2 if u[0] == "down" else 1), n, u[0]))
                elif n == MOE_AT[u[1]] + RING:
                    L = u[1]
                    m0 = MOE_AT[L]
                    with sp.Fori(1, GROUPS) as g:
                        for j in range(RING):
                            q, kind = j // 3, ("gu", "gu", "down")[j % 3]
                            done = "down_done" if kind == "down" else "gu_done"
                            expert_slot_freed(sp, L, done, 16 * L + 2 * g + (q - 1))
                            e = g * EPG + 2 * q + (j % 3 if kind == "gu" else 0)
                            for dst, src in expert_sources(L, e, m0 + j, kind):
                                sp.dma_start(dst, src).then_inc(sem(f"weights_in{(m0 + j) % RING}"), 16)

            o = out[0].rearrange("(i p) d -> i p d", p=P)
            for j in range(2):
                sp.wait_ge(sem("x_done_end"), j + 1)
                sp.dma_start(o[j], X[:, 2 + j, :]).then_inc(sem("out_stored"), 16)
            sp.wait_ge(sem("out_stored"), 32)

        @block.tensor
        def _(pe):
            pe.wait_ge(sem("rows_in"), 16 * 14)
            pe.wait_ge(sem("const_in"), 16)
            pe.transpose(bank[7][:, 0:128], rows[:, 0, :], ident)
            pe.transpose(bank[7][:, 128:252], rows[0:124, 1, :], ident[0:124, 0:124])
            pe.transpose(bank[7][:, 256:294], rows[0:NROWS3, 2, :], ident[0:NROWS3, 0:NROWS3]).then_inc(sem("par_turned"), 1)
            pe.wait_ge(sem("cs_ready"), 1)

            def mod_multiply(i):
                L, v = MOD_PAIRS[i]
                units = [where[("mod", L, v, h)] for h in (0, 1)]
                for n in units:
                    loaded(pe, n)
                if i:
                    pe.wait_ge(sem("mod_rows"), i)
                for k in range(KC):
                    for h in (0, 1):
                        at = 64 * h + 32 * (k % 2)
                        mm = pe.matmul(bank[6][at:at + 32, :], cs[:, k, :], slot(units[h])[:, k, :], start=k < 2, stop=k >= KC - 2)
                mm.then_inc(sem("mod_mm"), 1)

            def mod_turn(i):
                pe.wait_ge(sem("mod_rows"), i + 1)
                if i:
                    pe.wait_ge(sem("mod_cols"), i)
                for c in range(4):
                    mm = pe.matmul(bank[7][:, 4 * c:4 * c + 4], MR[:, i % 2, c * P:(c + 1) * P], C("sel"), start=True, stop=True)
                mm.then_inc(sem("mod_turned"), 1)

            def mod(i):
                mod_multiply(i)
                mod_turn(i)

            def turn_x(tag, tiles):
                for i in range(len(tiles) // 2):
                    pe.wait_ge(sem("xs"), 4 * nth(tag) + 2 * i + 2)
                    for k in range(KC):
                        u = KC * i + k
                        if u >= 4:
                            pe.wait_ge(sem(f"ht_{k % 2}"), 8 * nth(tag) + u // 2 - 1)
                        for j in range(2):
                            mm = pe.transpose(bank[u % 4][:, j * P:(j + 1) * P], XS[:, tiles[2 * i + j], k * P:(k + 1) * P], ident)
                        mm.then_inc(sem("turned"), 1)

            def gates(tag, L, v, streams, banks):
                n = 0
                for s in streams:
                    for h in range(2):
                        if n >= 2:
                            pe.wait_ge(sem("gate_rows"), gates_before(tag) + n - 1)
                        for c in range(4):
                            mm = pe.matmul(bank[banks[n % 2]][:, c * P:(c + 1) * P],
                                           mods[:, L, v, 4 * h + c, s:s + 1].to_broadcast([P, P]), ident, start=True, stop=True)
                        mm.then_inc(sem("gate_mms"), 1)
                        n += 1

            def project_out(L, lhs, tiles, first=0, between=None):
                for h in range(2):
                    n = where[("wout", L, h)]
                    w = slot(n)
                    loaded(pe, n)
                    for j, t in enumerate(tiles):
                        i = h * len(tiles) + j
                        if i >= 2:
                            pe.wait_ge(sem("out_used"), 8 * L + i - 1)
                        for k in range(KC):
                            mm = pe.matmul(bank[OUT_BANKS[L][i % 2]][:, :], lhs(k, j), w[:, (k + first) % KC, :], start=k == 0, stop=k == KC - 1)
                        mm.then_inc(sem("out_mm"), 1)
                        if between:
                            between(i)

            def route(L):
                nt, c, over, ntile = moe_plan(L)
                for i in range(2):
                    pe.wait_ge(sem(f"ht_{i}"), 8 * nth(f"m{L}") + (8, 4)[L])
                pe.wait_ge(sem("router_in"), 16)
                for k in range(KC):
                    mm = pe.matmul(bank[6][32 * (k % 4):32 * (k % 4) + 32, 0:nt * P], rw[:, k, :], hT[:, k, 0:nt * P], start=k < 4, stop=k >= 4)
                mm.then_inc(sem("logit_parts"), 1)
                pe.wait_ge(sem("logit_rows"), L + 1)
                for t in range(nt):
                    mm = pe.matmul(bank[2][:, t * 32:t * 32 + 32], MR[:, 0, t * P:(t + 1) * P], C("sel32"), start=True, stop=True)
                mm.then_inc(sem("logits"), 1)

                def h_rows(tiles):
                    for t in tiles:
                        for h in range(2):
                            i = 2 * t + h
                            if i >= 2:
                                pe.wait_ge(sem("h2_rows"), 8 * L + i - 1)
                            for k in range(4):
                                mm = pe.transpose(bank[3 + i % 2][:, k * P:(k + 1) * P], hT[:, 4 * h + k, t * P:(t + 1) * P], ident)
                            mm.then_inc(sem("h2_turned"), 1)

                h_rows(range(nt // 2))
                pe.wait_ge(sem("groups"), L + 1)
                G = routing(L)["G"]
                for t in range(nt):
                    for s in range(t + 1):
                        mm = pe.matmul(bank[5][:, 8 * t:8 * t + 8], C("lower") if s == t else C("ones"),
                                       G[:, 8 * s:8 * s + 8], start=s == 0, stop=s == t)
                for s in range(nt):
                    mm = pe.matmul(bank[5][:, 64:72], C("ones"), G[:, 8 * s:8 * s + 8], start=s == 0, stop=s == nt - 1)
                mm.then_inc(sem("ranks"), 1)
                h_rows(range(nt // 2, nt))
                pe.wait_ge(sem("onehot"), L + 1)
                for t in range(nt):
                    mm = pe.matmul(bank[6][:, 0:5 * ntile], onehot[:, t * P:(t + 1) * P],
                                   brhs[:, t * 5 * ntile:(t + 1) * 5 * ntile], start=t == 0, stop=t == nt - 1)
                mm.then_inc(sem("slots"), 1)
                pe.wait_ge(sem("h2_rows"), 8 * L + 2 * nt)
                if L == 1:
                    pe.wait_ge(sem("mod_cols"), 6 * L + 6)
                    gates("m1", 1, 5, (1,), (3, 4))
                pe.wait_ge(sem("gate_rows"), gates_before(f"m{L}") + (4, 2)[L])

            def experts(L):
                nt, c, over, ntile = moe_plan(L)
                m0 = MOE_AT[L]

                def body(g, tiles, skipped):
                    for s in tiles:
                        pe.wait_ge(sem(f"gathered_{s}"), 128 * L + 16 * g + 16)
                        if s:
                            pe.wait_ge(sem(f"hg_{s - 1}"), 8 * L + g + 1)
                        passed(pe)
                        for k in range(KC):
                            mm = pe.transpose(bank[0][:, k * ST:(k + 1) * ST], XG[s][:, k * P:(k + 1) * P], ident[0:ST, 0:ST])
                        mm.then_inc(sem(f"hg_turned_{s}"), 1)
                    for q in range(2):
                        for s in tiles:
                            if q == 0:
                                pe.wait_ge(sem(f"hg_{s}"), 8 * L + g + 1)
                            if s == 0:
                                for x in range(2):
                                    n = m0 + 3 * q + x
                                    pe.wait_ge(sem(f"weights_in{n % RING}"), 32 * g + 32 * (n // RING + 1))
                            pe.wait_ge(sem(f"he_{s}"), 16 * L + 2 * g + q + 1)
                            for k in range(KC):
                                for x in range(2):
                                    mm = pe.matmul(bank[1 + s][ST * x:ST * x + ST, :], HG[s][:, k, :],
                                                   slot(m0 + 3 * q + x)[:, k, :], start=k == 0, stop=k == KC - 1)
                            mm.then_inc(sem(f"gu_done_{s}"), 1)
                        n = m0 + 3 * q + 2
                        pe.wait_ge(sem(f"weights_in{n % RING}"), 32 * g + 32 * (n // RING + 1))
                        dn = ring[:, n % RING, :].rearrange("p (x f n) -> p x f n", x=2, f=2)
                        for s in tiles:
                            pe.wait_ge(sem(f"he_{s}"), 16 * L + 2 * g + q + 2)
                            if skipped and q == 0:
                                bump(pe, skipped)
                            for f in range(2):
                                mm = pe.transpose(bank[3 + s][:, f * P:(f + 1) * P], HE[s][:, f * P:(f + 1) * P], ident)
                            mm.then_inc(sem(f"he_turned_{s}"), 1)
                        for s in tiles:
                            pe.wait_ge(sem(f"het_{s}"), 16 * L + 2 * g + q + 1)
                            if q == 0:
                                pe.wait_ge(sem(f"y_rows_{s}"), 8 * L + g + 1)
                            for f in range(2):
                                for x in range(2):
                                    for h in range(2):
                                        mm = pe.matmul(bank[5 + s][ST * h:ST * h + ST, :], HET[s][:, f, ST * x:ST * x + ST],
                                                       dn[:, x, f, 512 * h:512 * h + 512],
                                                       start=q == 0 and f == 0 and x == 0, stop=q == 1 and f == 1 and x == 1)
                            mm.then_inc(sem(f"down_done_{s}"), 1)

                group_loop(pe, L, body, [("hg_turned_1", 1), ("gu_done_1", 2), ("he_turned_1", 2), ("down_done_1", 2)])

            for i in range(2):
                mod(i)
            turn_x("a0", range(4))
            for i in range(2):
                pe.wait_ge(sem(f"ht_{i}"), 8)
            for m in range(4):
                n = where[("win", m // 2)]
                w = slot(n)
                loaded(pe, n)
                for part in (1, 0):
                    b = bank[2 * (m % 2) + part]
                    if m >= 2:
                        pe.wait_ge(sem("glu_done"), m - 1)
                    for k in range(KC):
                        mm = pe.matmul(b[:, :], w[:, k, 256 * part + P * (m % 2):256 * part + P * (m % 2) + P], hT[:, k, :],
                                       start=k == 0, stop=k == KC - 1)
                    mm.then_inc(sem("value_mm" if part == 0 else "gate_mm"), 1)
            n = where[("win", 2)]
            w = slot(n)
            loaded(pe, n)
            for g in range(4):
                if g >= 2:
                    pe.wait_ge(sem("pool_in"), g - 1)
                for k in range(KC):
                    mm = pe.matmul(bank[4 + g % 2][:, :], w[:, k, P * g:P * g + P], hT[:, k, :], start=k == 0, stop=k == KC - 1)
                mm.then_inc(sem("pool_mm"), 1)
            mod(2)
            mod(3)
            pe.wait_ge(sem("pool_w_in"), 16)
            pe.wait_ge(sem("pooled"), 4)
            for g in range(4):
                if g == 0:
                    pe.wait_ge(sem("pool_in"), 4)
                if g >= 2:
                    pe.wait_ge(sem("pool_out"), g - 1)
                pe.matmul(bank[4 + g % 2][:, :], pw[:, g, :], mixT[:, g, :], start=True, stop=True).then_inc(sem("pool_mix"), 1)
            mod(4)
            pe.wait_ge(sem("conv_done"), 4)
            for t in range(NT):
                if t == 0:
                    pe.wait_ge(sem("glu_done"), 4)
                for m in range(4):
                    mm = pe.transpose(bank[t][:, m * P:(m + 1) * P], CV[:, m, t * P:(t + 1) * P], ident)
                mm.then_inc(sem("conv_turned"), 1)
            pe.wait_ge(sem("mod_cols"), 3)
            pe.wait_ge(sem("pool_out"), 4)
            gates("a0", 0, 2, (0, 1), (4, 5))
            mod(5)
            for m in range(4):
                if m == 0:
                    pe.wait_ge(sem("ln_rows"), 4)
                for t in range(NT):
                    mm = pe.transpose(bank[m][:, t * P:(t + 1) * P], LNS[:, t, m * P:(m + 1) * P], ident)
                mm.then_inc(sem("ln_turned"), 1)

            def mixed(k, j):
                m = (k + 4) % KC
                if j == 0 and m < 4:
                    pe.wait_ge(sem("mix_done"), m + 1)
                return mixT[:, m, j * P:(j + 1) * P]

            def layer1_mods(i):
                if i == 1:
                    mod_multiply(6)
                elif i == 2:
                    mod_turn(6)

            pe.wait_ge(sem("gate_rows"), 4)
            project_out(0, mixed, range(4), 4, layer1_mods)
            mod(7)
            gates("m0", 0, 5, (0, 1), (2, 3))
            mod(8)
            pe.wait_ge(sem("gate_rows"), gates_before("a1"))
            turn_x("m0", range(4))
            route(0)
            experts(0)
            overflow_pe(pe, 0)
            pe.wait_ge(sem("y_rows_1"), GROUPS + 1)
            mod(9)
            turn_x("a1", range(4))
            for i in range(2):
                pe.wait_ge(sem(f"ht_{i}"), 24)
            project_pe(pe, loaded, mod_multiply)
            attention_pe(pe)
            mod_turn(10)
            gates("a1", 1, 2, (1,), (4, 5))
            pe.wait_ge(sem("o_cols"), len(UNITS))
            project_out(1, lambda k, j: oT[:, k, j * P:(j + 1) * P], (2, 3))
            mod(11)
            turn_x("m1", (2, 3))
            route(1)
            experts(1)
            overflow_pe(pe, 1)

        @block.scalar
        def _(act):
            r1 = "(o p) -> o p"
            for r, n, src in ((R_CCTX, 8, a["c_ctx"].rearrange(r1, p=P)), (R_C, 8, a["c"][0].rearrange(r1, p=P)),
                              (R_DWB, 4, a["conv_dw_b"][0].rearrange(r1, p=P)), (R_LNG, 4, a["conv_ln_g"][0].rearrange(r1, p=P)),
                              (R_LNB, 4, a["conv_ln_b"][0].rearrange(r1, p=P)), (R_PSC, 4, a["pool_scale"][0].rearrange(r1, p=P)),
                              (R_GCQ, 2, a["mla_g_cq"][0].rearrange(r1, p=P)), (R_GCKV, 1, a["mla_g_ckv"]),
                              (R_SUBG, 1, a["diff_sub_g"]), (R_QN, 1, a["qk_g_mla"][0, 0:1, 0:P]), (R_KN, 1, a["qk_g_mla"][0, 1:2, 0:P])):
                act.dma_start(rows[r - 256:r - 256 + n, 2, :], src).then_inc(sem("rows_in"), 16)

            for s in range(2):
                act.sem_inc(sem(f"y_rows_{s}"), 1)

            act.wait_ge(sem("par_ready"), 1)
            act.activation(csg[:, :], par[:, R_CCTX:R_CCTX + 16], ACT.Sigmoid).then_inc(sem("cs_sig"), 1)

            def square_rows(tag):
                if tag == "a0":
                    act.wait_ge(sem("x_in"), 64)
                else:
                    act.wait_ge(sem(f"x_done_{tag}"), 1)
                for t in x_tiles(tag):
                    if tag == "a1" and t:
                        act.wait_ge(sem("x_done_a1"), t + 1)
                    act.activation(XS[:, t, :], X[:, t, :], ACT.Square,
                                   accum_out=ss[:, t:t + 1]).then_inc(sem("ss"), 1)

            def mod_copy(i):
                act.wait_ge(sem("mod_mm"), i + 1)
                act.activation(MR[:, i % 2, :], bank[6][:, :], ACT.Copy).then_inc(sem("mod_rows"), 1)

            def mod_columns(i):
                L, v = MOD_PAIRS[i]
                act.wait_ge(sem("mod_turned"), i + 1)
                for k in range(KC):
                    r, at = R_MODB + 48 * L + 8 * v + k, 4 * (k % 4) + 2 * (k // 4)
                    ins = act.activation(mods[:, L, v, k, :], bank[7][:, at:at + 2], ACT.Identity, bias=par[:, r:r + 1])
                ins.then_inc(sem("mod_cols"), 1)

            def mod_rows(i):
                mod_copy(i)
                mod_columns(i)

            def hcols(tag):
                L, n, v = norm_of(tag)
                act.wait_ge(sem("gsc"), 2 * L + n + 1)
                for i, (s, lo, hi) in enumerate(stream_cols(tag)):
                    for k in range(0, KC, 2):
                        u = KC * i + k
                        act.wait_ge(sem("turned"), 16 * nth(tag) + u + 1)
                        act.activation(hT[:, k, lo:hi], bank[u % 4][:, 0:HALF], ACT.Identity,
                                       bias=mods[:, L, v, k, s:s + 1], scale=gsc[:, L, n, k, s:s + 1]).then_inc(sem("ht_0"), 1)

            def gate_rows(tag, streams, banks):
                n = 0
                for s in streams:
                    for h in range(2):
                        act.wait_ge(sem("gate_mms"), gates_before(tag) + n + 1)
                        act.activation(GB[:, s, 512 * h:512 * h + 512], bank[banks[n % 2]][:, :], ACT.Copy)\
                           .then_inc(sem("gate_rows"), 1)
                        n += 1

            def experts(L):
                if L == 0:
                    act.activation(YO[1], X[:, 0, 0:512], ACT.Copy).then_inc(sem("filler"), 1)
                    act.wait_ge(sem("filler"), 1)

                def body(g, tiles, skipped):
                    for q in range(2):
                        for s in tiles:
                            act.wait_ge(sem(f"gu_done_{s}"), 16 * L + 2 * g + q + 1)
                            act.activation(SG[s], bank[1 + s][:, 0:DE], ACT.Sigmoid).then_inc(sem(f"sg_{s}"), 1)
                        for s in tiles:
                            act.wait_ge(sem(f"he_turned_{s}"), 16 * L + 2 * g + q + 1)
                            act.activation(HET[s].rearrange("p f s -> p (f s)"), bank[3 + s][:, 0:DE], ACT.Copy)\
                               .then_inc(sem(f"het_{s}"), 1)
                    for s in tiles:
                        act.wait_ge(sem(f"down_done_{s}"), 16 * L + 2 * g + 2)
                        act.wait_ge(sem(f"y_free_{s}"), 8 * L + g + 1)
                        act.activation(YO[s], bank[5 + s][:, :], ACT.Copy).then_inc(sem(f"y_rows_{s}"), 1)
                    if skipped:
                        bump(act, skipped)

                group_loop(act, L, body, [("sg_1", 2), ("het_1", 2), ("y_rows_1", 1)])

            mod_rows(0)
            square_rows("a0")
            mod_rows(1)
            hcols("a0")
            for m in range(4):
                act.wait_ge(sem("gate_mm"), m + 1)
                if m >= 2:
                    act.wait_ge(sem("glu_done"), m - 1)
                act.activation(SGL[m % 2], bank[2 * (m % 2) + 1][:, :], ACT.Sigmoid).then_inc(sem("glu_sig"), 1)
            act.wait_ge(sem("pads"), 2)
            for g in range(4):
                act.wait_ge(sem("pool_mm"), g + 1)
                act.activation(PP[:, g, :, PADP:PADP + HALF], bank[4 + g % 2][:, :].rearrange("p (s t) -> p s t", s=2), ACT.Copy)\
                   .then_inc(sem("pool_in"), 1)
            for i in range(2, 4):
                mod_rows(i)
            for g in range(4):
                act.wait_ge(sem("pool_mix"), g + 1)
                act.activation(mixT[:, 4 + g, :], bank[4 + g % 2][:, :], ACT.Identity, scale=par[:, R_PSC + g:R_PSC + g + 1])\
                   .then_inc(sem("pool_out"), 1)
            mod_rows(4)
            gate_rows("a0", (0, 1), (4, 5))
            mod_rows(5)
            for m in range(4):
                act.wait_ge(sem("ln_turned"), m + 1)
                if m >= 2:
                    act.wait_ge(sem("mix_done"), m - 1)
                gb = dict(bias=par[:, R_LNB + m:R_LNB + m + 1], scale=par[:, R_LNG + m:R_LNG + m + 1])
                act.activation(mixT[:, m, :], bank[m][:, :], ACT.Identity, **gb)
                act.activation(SGL[m % 2], bank[m][:, :], ACT.Sigmoid, **gb).then_inc(sem("ln_sig"), 1)
            mod_rows(6)
            square_rows("m0")
            mod_rows(7)
            act.wait_ge(sem("out_used"), 8)
            gate_rows("m0", (0, 1), (2, 3))
            mod_rows(8)
            hcols("m0")
            moe_scalar(act, 0, gate_rows, experts)
            mod_rows(9)
            square_rows("a1")
            hcols("a1")
            attention_scalar(act, mod_copy)
            mod_columns(10)
            gate_rows("a1", (1,), (4, 5))
            square_rows("m1")
            mod_copy(11)
            act.activation(lam[:, 6:7], lam[:, 2:3], ACT.Sigmoid)
            mod_columns(11)
            hcols("m1")
            moe_scalar(act, 1, gate_rows, experts)

        def attention_vector(dve, link):
            tt, ts, red = dve.tensor_tensor, dve.tensor_scalar, dve.tensor_reduce
            la = brow[:, B_LAM:B_LAM + 256].rearrange("p (a b d) -> p a b d", a=2, b=2)
            dve.wait_ge(sem("brow_in"), 64)
            dve.wait_ge(sem("ht_1"), 24)
            link(tt(lamp.rearrange("p (a d) -> p a d", a=2), la[:, :, 0, :], la[:, :, 1, :], ALU.mult))
            red(lam[:, 0:2], lamp.rearrange("p (a d) -> p a d", a=2), AX.X, ALU.add).then_inc(sem("lam_dots"), 1)
            ts(subs[:, 0:1], par[:, R_SUBG:R_SUBG + 1], 1.0 - LAM_INIT, None, ALU.mult).then_inc(sem("sub_scale"), 1)

            def rope(rows_, n, t, out_):
                r4 = rows_.rearrange("p (n a d) -> p n a d", n=n, a=2)
                cosb = C("cos", 32 * (t - 2), 32 * (t - 1)).unsqueeze(1).to_broadcast([P, 2 * n, 32])
                sinb = C("sin", 32 * (t - 2), 32 * (t - 1)).unsqueeze(1).to_broadcast([P, 2 * n, 32])
                flat = rows_.rearrange("p (n d) -> p n d", d=32)
                ac, as_ = RA[:, 0:64 * n], PT[1][:, 0:64 * n]
                tt(ac.rearrange("p (n d) -> p n d", d=32), flat, cosb, ALU.mult)
                link(tt(as_.rearrange("p (n d) -> p n d", d=32), flat, sinb, ALU.mult))
                c4 = ac.rearrange("p (n a d) -> p n a d", n=n, a=2)
                s4 = as_.rearrange("p (n a d) -> p n a d", n=n, a=2)
                o4 = out_.rearrange("p (n a d) -> p n a d", n=n, a=2)
                tt(o4[:, :, 0, :], c4[:, :, 0, :], s4[:, :, 1, :], ALU.subtract)
                return tt(o4[:, :, 1, :], c4[:, :, 1, :], s4[:, :, 0, :], ALU.add)

            RUNS = {"kd": (8, 64), "qd": (8, 64), "ckv": (1, 128), "ql": (1, 256), "qm": (2, 192), "kvm": (2, 128)}

            def sums(i):
                kind, t, p = ITEMS[i]
                c = count(i, NORMED)
                sq, q = SQ[c % 2], ssq[:, 8 * (c % 2):8 * (c % 2) + 8]
                nseg, wseg = RUNS[kind]
                dve.wait_ge(sem("item_act"), i + 1)
                if kind == "ckv":
                    red(ssr[:, t:t + 1], sq[:, 128:192], AX.X, ALU.add)
                ins = red(q[:, 0:nseg], sq[:, 0:nseg * wseg].rearrange("p (n d) -> p n d", n=nseg), AX.X, ALU.add)
                if kind == "kvm":
                    link(ins)
                    ins = ts(q[:, 0:2], q[:, 0:2], ssr[:, t:t + 1], None, ALU.add)
                ins.then_inc(sem("ssq_ready"), 1)

            def rows_of(i):
                kind, t, p = ITEMS[i]
                c = count(i, NORMED)
                src, qn, rt = bank[PBANK[i % 4]], QN[c % 2], RT[c % 2]
                nseg, wseg = RUNS[kind]
                r = rs[:, 8 * (c % 2):8 * (c % 2) + nseg]
                if c >= 2:
                    dve.wait_ge(sem("cols_turned"), c - 1)
                if kind == "ckv":
                    ts_k = KR[:, t, :]
                    link(tt(ts_k, src[:, 128:192], brow[:, B_QKM + 192 + 128:B_QKM + 384], ALU.mult))
                    if t >= 2:
                        link(rope(ts_k, 1, t, ts_k))
                dve.wait_ge(sem("rs_ready"), c + 1)
                rb_ = r.unsqueeze(2).to_broadcast([P, nseg, wseg])
                if kind == "kvm":
                    two = src[:, :].rearrange("p (h d) -> p h d", h=2)[:, :, 0:P]
                    tt(qn[:, 0:256].rearrange("p (h d) -> p h d", h=2), two, rb_, ALU.mult).then_inc(sem("item_dve"), 1)
                    tt(rt.rearrange("p (h d) -> p h d", h=2), KR[:, t, :].unsqueeze(1).to_broadcast([P, 2, 64]),
                       r.unsqueeze(2).to_broadcast([P, 2, 64]), ALU.mult).then_inc(sem("rows_done"), 1)
                    return
                ins = tt(qn[:, 0:nseg * wseg].rearrange("p (n d) -> p n d", n=nseg), src[:, 0:nseg * wseg].rearrange("p (n d) -> p n d", n=nseg), rb_, ALU.mult)
                ins.then_inc(sem("item_dve"), 1)
                dve.wait_ge(sem("item_dve"), c + 1)
                if kind in ("kd", "qd"):
                    g = brow[:, B_QKD + (64 if kind == "kd" else 0):B_QKD + (128 if kind == "kd" else 64)]
                    q3 = qn.rearrange("p (n d) -> p n d", n=8)
                    ins = tt(q3, q3, g.unsqueeze(1).to_broadcast([P, 8, 64]), ALU.mult)
                    if t >= 2:
                        link(ins)
                        ins = rope(qn, 8, t, qn)
                    ins.then_inc(sem("rows_done"), 1)
                elif kind == "qm":
                    link(tt(rt.rearrange("p (h d) -> p h d", h=2), qn[:, 0:384].rearrange("p (h d) -> p h d", h=2)[:, :, P:192],
                            brow[:, B_QKM + P:B_QKM + 192].unsqueeze(1).to_broadcast([P, 2, 64]), ALU.mult))
                    rope(rt, 2, t, rt).then_inc(sem("rows_done"), 1)
                else:
                    dve.nop()
                    dve.sem_inc(sem("rows_done"), 1)

            waiting = None
            for i, (kind, t, p) in enumerate(ITEMS):
                if kind == "vd":
                    continue
                sums(i)
                if waiting is not None:
                    rows_of(waiting)
                    waiting = None
                if kind in ("kd", "qd"):
                    rows_of(i)
                else:
                    waiting = i
            rows_of(waiting)

            dve.wait_ge(sem("lam_exp"), 1)
            link(tt(lam[:, 4:5], lam[:, 3:4], lam[:, 2:3], ALU.subtract))
            link(ts(lam[:, 5:6], lam[:, 4:5], -LAM_INIT, None, ALU.add))
            n_units = len(UNITS)
            def maxima(i):
                d = UNITS[i][0]
                dve.wait_ge(sem("score_mm"), i + 1)
                o = 2 * (i % 2)
                for m in range(1 + d):
                    ins = red(mx[:, o + m:o + m + 1], bank[o + m][:, :], AX.X, ALU.max)
                link(ins)
                ts(nb[:, o:o + 1 + d], mx[:, o:o + 1 + d], -(MLA_SCALE, DIFF_SCALE)[d], None, ALU.mult).then_inc(sem("max_done"), 1)

            def normalize(i):
                d = UNITS[i][0]
                o, u = 2 * (i % 2), 2 * (i % 4)
                dve.wait_ge(sem("exp_done"), i + 1)
                ins = dve.reciprocal(ri[:, u:u + 1 + d], es[:, o:o + 1 + d])
                if d:
                    link(ins)
                    tt(ri[:, u + 1:u + 2], ri[:, u + 1:u + 2], lam[:, 5:6], ALU.mult)
                    link(ts(EX[:, i % 2, 0, :], EX[:, i % 2, 0, :], ri[:, u:u + 1], None, ALU.mult))
                    ins = dve.scalar_tensor_tensor(out=EX[:, i % 2, 0, :], in0=EX[:, i % 2, 1, :], scalar=ri[:, u + 1:u + 2],
                                                   in1=EX[:, i % 2, 0, :], op0=ALU.mult, op1=ALU.add)
                ins.then_inc(sem("probs_ready"), 1)

            def output_rows(i):
                dve.wait_ge(sem("pv_mm"), i + 1)
                if UNITS[i][0]:
                    dve.wait_ge(sem("o_rstd"), i - 7)
                    scale = ors[:, i % 2:i % 2 + 1]
                else:
                    dve.wait_ge(sem("probs_ready"), i + 1)
                    scale = ri[:, 2 * (i % 4):2 * (i % 4) + 1]
                if i >= 2:
                    dve.wait_ge(sem("o_turned"), i - 1)
                ts(OR[i % 2], bank[5][:, 0:P], scale, None, ALU.mult).then_inc(sem("o_rows"), 1)

            for i in range(n_units + 2):
                if i < n_units:
                    maxima(i)
                if i >= 2:
                    output_rows(i - 2)
                if i < n_units:
                    normalize(i)

        @block.vector
        def _(dve):
            link = Chain(dve, "vector_chain")
            tt, ts, red = dve.tensor_tensor, dve.tensor_scalar, dve.tensor_reduce

            dve.memset(cs[:, :, :], 0.0)
            dve.memset(YP[:, :, :, 0:PADC], 0.0)
            dve.memset(YP[:, :, :, PADC + HALF:], 0.0).then_inc(sem("pads"), 1)
            dve.memset(PP[:, :, :, 0:PADP], 0.0)
            dve.memset(PP[:, :, :, PADP + HALF:], 0.0).then_inc(sem("pads"), 1)
            dve.wait_ge(sem("pads"), 2)
            dve.wait_ge(sem("par_turned"), 1)
            dve.tensor_copy(par[:, 0:252], bank[7][:, 0:252])
            dve.tensor_copy(par[:, 256:294], bank[7][:, 256:294]).then_inc(sem("par_ready"), 1)
            dve.wait_ge(sem("par_ready"), 1)
            dve.wait_ge(sem("cs_sig"), 1)
            tt(cs[:, :, 0:2].rearrange("p k s -> p s k"), csg.rearrange("p (s k) -> p s k", s=2),
               par[:, R_CCTX:R_CCTX + 16].rearrange("p (s k) -> p s k", s=2), ALU.mult).then_inc(sem("cs_ready"), 1)

            def norm_scale(L, n):
                dve.wait_ge(sem("mod_cols"), 6 * L + (2 if n == 0 else 5))
                g = par[:, R_NORM + 16 * L + 8 * n:R_NORM + 16 * L + 8 * n + 8]
                for s in range(2):
                    ins = dve.scalar_tensor_tensor(out=gsc[:, L, n, :, s], in0=mods[:, L, 3 * n + 1, :, s], scalar=1.0, in1=g, op0=ALU.add, op1=ALU.mult)
                ins.then_inc(sem("gsc"), 1)

            def norm_rows(tag):
                L, n, v = norm_of(tag)
                t = x_tiles(tag)
                for i in range(len(t) // 2):
                    dve.wait_ge(sem("rstd"), 2 * nth(tag) + i + 1)
                    for j in t[2 * i:2 * i + 2]:
                        ts(XS[:, j, :], X[:, j, :], rstd[:, j:j + 1], None, ALU.mult).then_inc(sem("xs"), 1)
                dve.wait_ge(sem("gsc"), 2 * L + n + 1)
                for i, (s, lo, hi) in enumerate(stream_cols(tag)):
                    for k in range(1, KC, 2):
                        u = KC * i + k
                        dve.wait_ge(sem("turned"), 16 * nth(tag) + u + 1)
                        ts(hT[:, k, lo:hi], bank[u % 4][:, 0:HALF], gsc[:, L, n, k, s:s + 1], mods[:, L, v, k, s:s + 1],
                           ALU.mult, ALU.add).then_inc(sem("ht_1"), 1)

            def add_out(L, streams):
                nj = 2 * len(streams)
                dve.wait_ge(sem("gate_rows"), gates_before(f"a{L}") + 2 * len(streams))
                for h in range(2):
                    for j in range(nj):
                        i = h * nj + j
                        dve.wait_ge(sem("out_mm"), 8 * L + i + 1)
                        if i >= 2:
                            dve.wait_ge(sem("x_added"), 8 * L + i - 1)
                        tt(OUTT[i % 2], bank[OUT_BANKS[L][i % 2]][:, :], GB[:, streams[j // 2], 512 * h:512 * h + 512], ALU.mult).then_inc(sem("out_used"), 1)

            def route(L):
                nt, c, over, ntile = moe_plan(L)
                r = routing(L)
                dve.wait_ge(sem("scored"), L + 1)
                link(tt(r["biased"].rearrange("p (t e) -> p t e", t=nt), r["score"].rearrange("p (t e) -> p t e", t=nt),
                        brow[:, B_RB:B_RB + 32].unsqueeze(1).to_broadcast([P, nt, 32]), ALU.add))
                b4 = r["biased"].rearrange("p (g a b) -> p g a b", a=2, b=2)
                hi = r["hl"][:, 0:nt * 16].rearrange("p (g a) -> p g a", a=2)
                lo = r["hl"][:, nt * 16:nt * 32].rearrange("p (g a) -> p g a", a=2)
                m1, m2, m3 = (r["m12"][:, nt * 8 * i:nt * 8 * i + nt * 8] for i in range(3))
                tt(hi, b4[:, :, :, 0], b4[:, :, :, 1], ALU.max)
                link(tt(lo, b4[:, :, :, 0], b4[:, :, :, 1], ALU.min))
                tt(m1, hi[:, :, 0], hi[:, :, 1], ALU.max)
                tt(m2, hi[:, :, 0], hi[:, :, 1], ALU.min)
                link(tt(m3, lo[:, :, 0], lo[:, :, 1], ALU.max))
                link(tt(m2, m2, m3, ALU.max))
                link(tt(r["gs"], m1, m2, ALU.add))
                v8 = lambda x: x.rearrange("p (t g) -> p t g", t=nt)
                over8 = lambda x: x.unsqueeze(2).to_broadcast([P, nt, 8])
                link(red(r["gm"], v8(r["gs"]), AX.X, ALU.max))
                link(tt(v8(m1), v8(r["gs"]), over8(r["gm"]), ALU.is_equal))
                link(tt(v8(m2), v8(m1), C("gdown").unsqueeze(1).to_broadcast([P, nt, 8]), ALU.mult))
                link(red(r["gm"], v8(m2), AX.X, ALU.max))
                G = r["G"]
                tt(v8(G), v8(m2), over8(r["gm"]), ALU.is_equal).then_inc(sem("groups"), 1)
                dve.wait_ge(sem("groups"), L + 1)
                for src, dst in ((r["biased"], r["sel4"]), (r["score"], r["sc1"])):
                    link(tt(big[:, 0:nt * 32].rearrange("p (g e) -> p g e", e=4), src.rearrange("p (g e) -> p g e", e=4),
                            G.unsqueeze(2).to_broadcast([P, nt * 8, 4]), ALU.mult))
                    link(red(dst[:, 0:nt * 4].rearrange("p (t e) -> p t e", t=nt),
                             big[:, 0:nt * 32].rearrange("p (t g e) -> p t e g", t=nt, g=8), AX.X, ALU.add))
                s4 = r["sel4"][:, 0:nt * 4].rearrange("p (t e) -> p t e", t=nt)
                cmp_ = big[:, 0:nt * 16].rearrange("p (t e j) -> p t e j", t=nt, e=4)
                eq_ = big[:, 64:64 + nt * 16].rearrange("p (t e j) -> p t e j", t=nt, e=4)
                sj = s4.unsqueeze(2).to_broadcast([P, nt, 4, 4])
                se = s4.unsqueeze(3).to_broadcast([P, nt, 4, 4])
                tt(cmp_, sj, se, ALU.is_gt)
                link(tt(eq_, sj, se, ALU.is_equal))
                link(tt(eq_.rearrange("p t e j -> p t (e j)"), eq_.rearrange("p t e j -> p t (e j)"),
                        C("tie").unsqueeze(1).to_broadcast([P, nt, 16]), ALU.mult))
                link(tt(cmp_.rearrange("p t e j -> p (t e j)"), cmp_.rearrange("p t e j -> p (t e j)"), eq_.rearrange("p t e j -> p (t e j)"), ALU.add))
                w4 = r["w4"][:, 0:nt * 4]
                link(red(w4, cmp_.rearrange("p t e j -> p (t e) j"), AX.X, ALU.add))
                link(dve.scalar_tensor_tensor(out=w4, in0=w4, scalar=2.0, in1=r["sc1"][:, 0:nt * 4], op0=ALU.is_lt, op1=ALU.mult))
                w4t = w4.rearrange("p (t e) -> p t e", t=nt)
                link(red(r["wsum"], w4t, AX.X, ALU.add))
                link(dve.reciprocal(r["winv"], r["wsum"]))
                link(tt(w4t, w4t, r["winv"].unsqueeze(2).to_broadcast([P, nt, 4]), ALU.mult))
                dve.wait_ge(sem("ranks"), L + 1)
                nthr = nt * 2 - 1
                link(tt(big[:, 0:nt * 8], bank[5][:, 0:nt * 8], G, ALU.mult))
                link(red(r["rank"], v8(big[:, 0:nt * 8]), AX.X, ALU.add))
                no = nthr - (c - 1)
                link(tt(big[:, 0:8 * no].rearrange("p (g s) -> p g s", g=8), bank[5][:, 64:72].unsqueeze(2).to_broadcast([P, 8, no]),
                        C("thr", c - 1, nthr).unsqueeze(1).to_broadcast([P, 8, no]), ALU.is_gt))
                link(red(r["ov"], big[:, 0:8 * no].rearrange("p (g s) -> p g s", g=8), AX.X, ALU.add))
                link(tt(big[:, 0:64].rearrange("p (g j) -> p g j", g=8), C("before").rearrange("p (g j) -> p g j", g=8),
                        r["ov"].unsqueeze(1).to_broadcast([P, 8, 8]), ALU.mult))
                link(red(r["excl"], big[:, 0:64].rearrange("p (g j) -> p g j", g=8), AX.X, ALU.add))
                link(tt(big[:, 0:nt * nthr].rearrange("p (t s) -> p t s", t=nt), r["rank"].unsqueeze(2).to_broadcast([P, nt, nthr]),
                        C("thr", 0, nthr).unsqueeze(1).to_broadcast([P, nt, nthr]), ALU.is_ge))
                link(red(r["q"], big[:, 0:nt * nthr].rearrange("p (t s) -> p t s", t=nt), AX.X, ALU.add))
                link(dve.scalar_tensor_tensor(out=r["m"], in0=r["q"], scalar=-64.0, in1=r["rank"], op0=ALU.mult, op1=ALU.add))
                link(ts(r["isov"], r["q"], float(c), None, ALU.is_ge))
                for i, vec in enumerate((r["excl"], C("gup"))):
                    link(tt(v8(big[:, 0:nt * 8]), v8(G), vec.unsqueeze(1).to_broadcast([P, nt, 8]), ALU.mult))
                    link(red(r["tmp"][:, i * nt:(i + 1) * nt], v8(big[:, 0:nt * 8]), AX.X, ALU.add))
                ex, gid = r["tmp"][:, 0:nt], r["tmp"][:, nt:2 * nt]
                link(dve.scalar_tensor_tensor(out=ex, in0=gid, scalar=-float(c), in1=ex, op0=ALU.mult, op1=ALU.add))
                link(dve.scalar_tensor_tensor(out=ex, in0=ex, scalar=7.0 * c, in1=r["isov"], op0=ALU.add, op1=ALU.mult))
                link(dve.scalar_tensor_tensor(out=r["tile"], in0=gid, scalar=float(c), in1=r["q"], op0=ALU.mult, op1=ALU.add))
                link(tt(r["tile"], r["tile"], ex, ALU.add))
                link(dve.scalar_tensor_tensor(out=r["posf"], in0=r["tile"], scalar=float(ST), in1=r["m"], op0=ALU.mult, op1=ALU.add))
                vals = big[:, 0:5 * nt].rearrange("p (t v) -> p t v", t=nt)
                mask = big[:, 32:32 + nt * ntile].rearrange("p (t n) -> p t n", t=nt)
                dve.tensor_copy(vals[:, :, 0:1], C("tok", 0, nt).unsqueeze(2))
                dve.tensor_copy(vals[:, :, 1:5], w4[:, 0:4 * nt].rearrange("p (t e) -> p t e", e=4))
                tt(onehot[:, 0:nt * P].rearrange("p (t s) -> p t s", t=nt), C("iota64").unsqueeze(1).to_broadcast([P, nt, P]),
                   r["m"].unsqueeze(2).to_broadcast([P, nt, P]), ALU.is_equal)
                link(tt(mask, C("iota", 0, ntile).unsqueeze(1).to_broadcast([P, nt, ntile]),
                        r["tile"].unsqueeze(2).to_broadcast([P, nt, ntile]), ALU.is_equal))
                for t in range(nt):
                    o = t * 5 * ntile
                    ins = tt(brhs[:, o:o + 5 * ntile].rearrange("p (v n) -> p v n", v=5), mask[:, t].unsqueeze(1).to_broadcast([P, 5, ntile]),
                             vals[:, t].unsqueeze(2).to_broadcast([P, 5, ntile]), ALU.mult)
                ins.then_inc(sem("onehot"), 1)
                if c == 2:
                    ts(smalli[:, 40:48], bank[5][:, 64:72], float(ST), None, ALU.is_gt)
                dve.tensor_copy(smalli[:, 0:nt], r["posf"])
                link(tt(r["excl"], r["excl"], r["ov"], ALU.add))
                link(tt(big[:, 0:8 * over].rearrange("p (j g) -> p j g", g=8), r["excl"].unsqueeze(1).to_broadcast([P, over, 8]),
                        C("iota", 0, over).unsqueeze(2).to_broadcast([P, over, 8]), ALU.is_le))
                link(red(r["gov"][:, 0:over], big[:, 0:8 * over].rearrange("p (j g) -> p j g", g=8), AX.X, ALU.add))
                ts(smalli[:, 26:26 + over], r["gov"][:, 0:over], float(GROUPS - 1), None, ALU.min)
                dve.tensor_copy(smalli[:, 33:34], r["excl"][:, 7:8])
                dve.wait_ge(sem("slots"), L + 1)
                for x in range(2):
                    dve.tensor_copy(cwt[ST * x:ST * x + ST, 0:2 * ntile].rearrange("p (n q) -> p q n", q=2),
                                    bank[6][ST * x:ST * x + ST, ntile:5 * ntile].rearrange("p (q x n) -> p x q n", q=2, x=2)[:, x])
                dve.tensor_copy(smalli[:, 4:4 + ntile], bank[6][:, 0:ntile]).then_inc(sem("slots_ready"), 1)

            def experts(L):
                c = moe_plan(L)[1]

                def body(g, tiles, skipped):
                    for s in tiles:
                        dve.wait_ge(sem(f"hg_turned_{s}"), 8 * L + g + 1)
                        dve.tensor_copy(HG[s].rearrange("p k s -> p (k s)"), bank[0][:, :]).then_inc(sem(f"hg_{s}"), 1)
                    for q in range(2):
                        for s in tiles:
                            dve.wait_ge(sem(f"sg_{s}"), 16 * L + 2 * g + q + 1)
                            dve.scalar_tensor_tensor(out=T1[s], in0=SG[s], scalar=cwt[:, bass.ds(2 * c * g + (2 * s + q), 1)],
                                                     in1=bank[1 + s][:, 0:DE], op0=ALU.mult, op1=ALU.mult).then_inc(sem(f"t1_{s}"), 1)
                            dve.wait_ge(sem(f"t1_{s}"), 16 * L + 2 * g + q + 1)
                            dve.tensor_tensor(HE[s], T1[s], bank[1 + s][:, DE:2 * DE], ALU.mult).then_inc(sem(f"he_{s}"), 1)
                    if skipped:
                        bump(dve, skipped)

                group_loop(dve, L, body, [("hg_1", 1), ("t1_1", 2), ("he_1", 2)])

            def add_moe(L):
                nt = moe_plan(L)[0]
                dve.wait_ge(sem("gate_rows"), gates_before(f"m{L}") + (4, 2)[L])
                for j in range(nt):
                    t = j if L == 0 else 2 + j
                    yg = B[:, j * D:(j + 1) * D]
                    dve.wait_ge(sem(f"y_gathered_{j // 2 if L == 0 else j}"), 32 if L == 0 else 48)
                    link(tt(yg, yg, GB[:, t // 2, :], ALU.mult))
                    tt(X[:, t, :], X[:, t, :], yg, ALU.add).then_inc(sem("x_done_a1" if L == 0 else "x_done_end"), 1)

            for s in range(2):
                dve.sem_inc(sem(f"he_{s}"), 1)
            norm_scale(0, 0)
            norm_rows("a0")
            for m in range(4):
                dve.wait_ge(sem("glu_sig"), m + 1)
                dve.wait_ge(sem("value_mm"), m + 1)
                s3 = lambda x: x.rearrange("p (s t) -> p s t", s=2)
                tt(YP[:, m, :, PADC:PADC + HALF], s3(bank[2 * (m % 2)][:, :]), s3(SGL[m % 2]), ALU.mult).then_inc(sem("glu_done"), 1)
                dve.wait_ge(sem("glu_done"), m + 1)
                for j in range(TAPS):
                    col = R_TAPS + 4 * j + m
                    src, w, acc = YP[:, m, :, j:j + HALF], par[:, col:col + 1], s3(ACC[j % 2])
                    if j >= 2:
                        dve.wait_ge(sem("tap_done"), m * TAPS + j - 1)
                    if j == 0:
                        ins = ts(acc, src, w, par[:, R_DWB + m:R_DWB + m + 1], ALU.mult, ALU.add)
                    elif j == 1:
                        ins = ts(acc, src, w, None, ALU.mult)
                    else:
                        ins = dve.scalar_tensor_tensor(out=acc, in0=src, scalar=w, in1=acc, op0=ALU.mult, op1=ALU.add)
                    ins.then_inc(sem("tap_done"), 1)
                dve.wait_ge(sem("tap_done"), (m + 1) * TAPS)
                tt(CV[:, m, :], ACC[0], ACC[1], ALU.add).then_inc(sem("conv_done"), 1)
                dve.wait_ge(sem("conv_done"), m + 1)
            for t in range(NT):
                dve.wait_ge(sem("conv_turned"), t + 1)
                link(dve.bn_stats(stats[:, 6 * t:6 * t + 6], bank[t][:, :]))
                dve.bn_aggr(mv[:, 2 * t:2 * t + 2], stats[:, 6 * t:6 * t + 6]).then_inc(sem("ln_stats"), 1)
            dve.wait_ge(sem("ln_rstd"), 1)
            for t in range(NT):
                ts(LNS[:, t, :], bank[t][:, :], mv[:, 2 * t:2 * t + 1], lrs[:, t:t + 1], ALU.subtract, ALU.mult).then_inc(sem("ln_rows"), 1)
            for m in range(4):
                dve.wait_ge(sem("ln_sig"), m + 1)
                tt(mixT[:, m, :], mixT[:, m, :], SGL[m % 2], ALU.mult).then_inc(sem("mix_done"), 1)
            add_out(0, (0, 1))
            norm_scale(0, 1)
            norm_rows("m0")
            route(0)
            experts(0)
            overflow_vector(dve, 0)
            add_moe(0)
            norm_scale(1, 0)
            norm_rows("a1")
            attention_vector(dve, link)
            add_out(1, (1,))
            norm_scale(1, 1)
            norm_rows("m1")
            route(1)
            experts(1)
            overflow_vector(dve, 1)
            add_moe(1)

        @block.gpsimd
        def _(pool):
            link = Chain(pool, "pool_chain")
            for s in range(2):
                pool.sem_inc(sem(f"y_free_{s}"), 1)

            pool.dma_start(cst[:, :], a["const"][:, 0:NCONST - 4 * HALF]).then_inc(sem("const_in"), 16)

            def power(dst, src, n, scale, name):
                link(pool.tensor_scalar(dst, src, scale, EPS, ALU.mult, ALU.add))
                pool.tensor_tensor(dst, dst, C("half", 0, 1).to_broadcast([P, n]), ALU.pow).then_inc(sem(name), 1)

            def rstd_of(tag):
                t = x_tiles(tag)
                for i in range(len(t) // 2):
                    pool.wait_ge(sem("ss"), 4 * nth(tag) + 2 * i + 2)
                    power(rstd[:, t[2 * i]:t[2 * i] + 2], ss[:, t[2 * i]:t[2 * i] + 2], 2, 1.0 / D, "rstd")

            def add_out(L, tiles):
                for h in range(2):
                    for j, t in enumerate(tiles):
                        i = h * len(tiles) + j
                        pool.wait_ge(sem("out_used"), 8 * L + i + 1)
                        x = X[:, t, 512 * h:512 * h + 512]
                        pool.tensor_tensor(x, x, OUTT[i % 2], ALU.add).then_inc(sem("x_added"), 1)
                pool.wait_ge(sem("x_added"), 8 * L + 2 * len(tiles))
                pool.sem_inc(sem(f"x_done_m{L}"), 1)

            def experts(L):
                nt, c, over, ntile = moe_plan(L)
                for t in range(nt):
                    pool.wait_ge(sem("h2_rows"), 8 * L + 2 * t + 2)
                    pool.dma_start(h2d[t * P:(t + 1) * P, :], B[:, t * D:(t + 1) * D]).then_inc(sem("h2_stored"), 16)
                pool.wait_ge(sem("h2_stored"), 64 * L + 16 * nt)
                pool.wait_ge(sem("slots_ready"), L + 1)

                def store(g):
                    for s in range(c):
                        pool.wait_ge(sem(f"y_rows_{s}"), 8 * L + g + 2)
                        r = (g * c + s) * ST
                        for h in range(2):
                            pool.dma_start(yd[r:r + ST, 512 * h:512 * h + 512], YO[s][ST * h:ST * h + ST, :]).then_inc(sem(f"y_stored_{s}"), 16)

                def free(g):
                    for s in range(c):
                        pool.wait_ge(sem(f"y_stored_{s}"), 256 * L + 32 * g + 32)
                        pool.sem_inc(sem(f"y_free_{s}"), 1)

                for g in range(GROUPS):
                    for s in range(c):
                        if g:
                            pool.wait_ge(sem(f"gathered_{s}"), 128 * L + 16 * g)
                            pool.wait_ge(sem(f"hg_turned_{s}"), 8 * L + g)
                        i = 4 + g * c + s
                        pool.indirect_dma_start(XG[s], None, h2d[:, :], bass.IndirectOffsetOnAxis(ap=smalli[0:ST, i:i + 1], axis=0))\
                            .then_inc(sem(f"gathered_{s}"), 16)
                    if g >= 2:
                        free(g - 2)
                    if g:
                        store(g - 1)
                free(GROUPS - 2)
                store(GROUPS - 1)
                free(GROUPS - 1)
                overflow_pool(pool, L)
                for j in range(nt):
                    pool.indirect_dma_start(B[:, j * D:(j + 1) * D], None, yd[:, :], bass.IndirectOffsetOnAxis(ap=smalli[:, j:j + 1], axis=0))\
                        .then_inc(sem(f"y_gathered_{j // 2 if L == 0 else j}"), 16)

            pool.wait_ge(sem("const_in"), 16)
            rstd_of("a0")
            pool.dma_start(rw[:, :, :], a["router_w"].rearrange("(k p) e -> p k e", p=P)).then_inc(sem("router_in"), 16)
            pool.dma_start(pw[:, :, :], a["pool_w"][0].rearrange("g c d -> c g d")).then_inc(sem("pool_w_in"), 16)
            for at, src in ((B_RB, a["router_b"]), (B_QKM, a["qk_g_mla"][0].rearrange("a d -> (a d)")),
                            (B_QKD, a["qk_g_diff"][0].rearrange("a d -> (a d)")), (B_LAM, a["diff_lambda"][0].rearrange("a d -> (a d)"))):
                n = src.shape[0]
                pool.dma_start(brow[:, at:at + n], src.partition_broadcast(P)).then_inc(sem("brow_in"), 16)
            pool.wait_ge(sem("turned"), 2 * KC)
            invcnt = B[:, 2048:2048 + 4 * HALF]
            pool.dma_start(invcnt, a["const"][:, NCONST - 4 * HALF:]).then_inc(sem("counts_in"), 16)
            pool.wait_ge(sem("counts_in"), 16)
            pool.wait_ge(sem("x_in"), 64)
            for t in range(3):
                r = GROUPS * 2 * ST + t * P
                pool.dma_start(yd[r:r + P, :], X[:, t, :]).then_inc(sem("y_filled"), 16)
            for g, w in enumerate(WINDOWS):
                pool.wait_ge(sem("pool_in"), g + 1)
                if g:
                    pool.wait_ge(sem("pooled"), g)
                src, k, width = PP[:, g, :, :], 1, 2 * PADP + HALF
                while k < w:
                    width -= k
                    dst = TA if src is not TA else TB
                    link(pool.tensor_tensor(dst[:, :, 0:width], src[:, :, 0:width], src[:, :, k:k + width], ALU.add))
                    src, k = dst, 2 * k
                dst = TA if src is not TA else TB
                s3 = mixT[:, g, :].rearrange("p (s t) -> p s t", s=2)
                link(pool.tensor_tensor(dst[:, :, 0:HALF], src[:, :, PADP - w // 2:PADP - w // 2 + HALF],
                                        invcnt[:, g * HALF:(g + 1) * HALF].unsqueeze(1).to_broadcast([P, 2, HALF]), ALU.mult))
                pool.tensor_tensor(s3, dst[:, :, 0:HALF], PP[:, g, :, PADP:PADP + HALF], ALU.subtract).then_inc(sem("pooled"), 1)
            pool.wait_ge(sem("ln_stats"), NT)
            link(pool.tensor_scalar(lrs[:, :], mv.rearrange("p (t a) -> p a t", a=2)[:, 1], EPS, None, ALU.add))
            pool.tensor_tensor(lrs[:, :], lrs[:, :], C("half", 0, 1).to_broadcast([P, 4]), ALU.pow).then_inc(sem("ln_rstd"), 1)
            pool.wait_ge(sem("y_filled"), 48)
            add_out(0, (0, 1, 2, 3))
            rstd_of("m0")
            experts(0)
            rstd_of("a1")
            for i, (kind, t, p) in enumerate(ITEMS):
                if kind == "vd":
                    continue
                c = count(i, NORMED)
                n = {"kd": 8, "qd": 8, "ckv": 1, "ql": 1, "qm": 2, "kvm": 2}[kind]
                w = {"kd": 64, "qd": 64, "ckv": 128, "ql": 256, "qm": 192, "kvm": 192}[kind]
                pool.wait_ge(sem("ssq_ready"), c + 1)
                r = rs[:, 8 * (c % 2):8 * (c % 2) + n]
                power(r, ssq[:, 8 * (c % 2):8 * (c % 2) + n], n, 1.0 / w, "rs_ready")
            for i, (d, h, t) in enumerate(UNITS):
                if d:
                    pool.wait_ge(sem("o_squares"), i - 7)
                    power(ors[:, i % 2:i % 2 + 1], oss[:, i % 2:i % 2 + 1], 1, 1.0 / P, "o_rstd")
            add_out(1, (2, 3))
            rstd_of("m1")
            experts(1)


_INS = ["x", "c", "ctx", "c_ctx", "mod_w", "mod_b", "norm_g", "even_w_in", "conv_dw_w", "conv_dw_b", "conv_ln_g", "conv_ln_b",
        "pool_w", "pool_scale", "even_w_out", "odd_w_in", "mla_g_cq", "mla_w_uq", "mla_g_ckv", "mla_w_ukv", "qk_g_mla", "qk_g_diff",
        "diff_lambda", "diff_sub_g", "odd_w_out", "router_w", "router_b", "moe_w_gate", "moe_w_up", "moe_w_down"]


def kernel(**inputs):
    import concourse.bacc as bacc
    from concourse.bass_utils import run_bass_kernel_spmd

    nc = bacc.Bacc("TRN2", target_bir_lowering=False, num_devices=1)
    arrays, aps = {}, {}
    for name in _INS + ["const"]:
        v = constants() if name == "const" else np.ascontiguousarray(inputs[name])
        arrays[f"in_{name}"] = v
        aps[name] = nc.dram_tensor(f"in_{name}", v.shape, mybir.dt.from_np(v.dtype), kind="ExternalInput").ap()
    out = nc.dram_tensor("latents", (1, HALF, D), F32, kind="ExternalOutput").ap()
    generator_kernel(nc, aps, out)
    r = run_bass_kernel_spmd(nc, [arrays], core_ids=[0])
    return r.results[0]["latents"]
```
